# Optimizing a Trainium2 kernel written in Bass

```python
import jax, jax.numpy as jnp
from jax import lax
import numpy as np

D_MODEL = 1024
BATCH = 1
SEQ = 1024
DEPTH = 1
DEC_BATCH = 8
DEC_SEQ = 4
PAST_LEN = 2048
PAGE_SIZE = 128

A_HEADS = 4
A_DK = 128
A_DV = 128
A_WIDTH = A_HEADS * A_DK
A_CHUNK = 64
ATT_GROUPS = ((128, 1), (512, 4), (2048, 16))
N_GROUPS = 3
G_HEADS = 4
HEAD_DIM = 128
ATT_WIDTH = N_GROUPS * G_HEADS * HEAD_DIM
ATT_BLOCK = 128
ROT_DIM = HEAD_DIM // 4
ROPE_THETA = 500000.0
SPLITS = (A_WIDTH, 2 * A_WIDTH, 3 * A_WIDTH, 4 * A_WIDTH,
          4 * A_WIDTH + ATT_WIDTH, 4 * A_WIDTH + 2 * ATT_WIDTH, 4 * A_WIDTH + 3 * ATT_WIDTH)
IN_COLS = 4 * A_WIDTH + 3 * ATT_WIDTH + 2 * D_MODEL
P_HEADS = 8
N_KEYS = 128
N_EXPERTS = N_KEYS * N_KEYS
P_QDIM = 256
P_HALF = P_QDIM // 2
P_TOPK = 16
P_BLOCK = 256
EPS = 1e-6

kernel_name = "hgrn2_dilated_window_peer_adaln_step"

def rms_norm(x, w):
    xf = x.astype(jnp.float32)
    y = xf * lax.rsqrt(jnp.mean(xf * xf, axis=-1, keepdims=True) + EPS)
    return (y * w.astype(jnp.float32)).astype(x.dtype)

def partial_rope(x, pos):
    inv = ROPE_THETA ** (-jnp.arange(0, ROT_DIM, 2, dtype=jnp.float32) / ROT_DIM)
    ang = pos.astype(jnp.float32)[:, None] * inv[None, :]
    cos, sin = jnp.cos(ang), jnp.sin(ang)
    xr = x[..., :ROT_DIM].astype(jnp.float32)
    x1, x2 = xr[..., :ROT_DIM // 2], xr[..., ROT_DIM // 2:]
    rot = jnp.concatenate([x1 * cos - x2 * sin, x1 * sin + x2 * cos], axis=-1)
    return jnp.concatenate([rot.astype(x.dtype), x[..., ROT_DIM:]], axis=-1)

def hgrn_chunked(q, k, v, logf, S0):
    B, T, H, _ = q.shape
    dv = v.shape[-1]
    C = min(A_CHUNK, T)
    pad = (-T) % C
    N = (T + pad) // C

    def blocks(a):
        a = jnp.pad(a.astype(jnp.float32), ((0, 0), (0, pad), (0, 0), (0, 0)))
        return a.reshape(B, N, C, H, a.shape[-1]).transpose(1, 0, 3, 2, 4)

    qc, kc, vc, gc = blocks(q), blocks(k), blocks(v), blocks(logf)
    causal = jnp.tril(jnp.ones((C, C), dtype=bool))[:, :, None]

    def step(S, inp):
        qb, kb, vb, gb = inp
        b = jnp.cumsum(gb, axis=2)
        decay = jnp.exp(jnp.where(causal, b[:, :, :, None, :] - b[:, :, None, :, :], -jnp.inf))
        A = jnp.einsum('bhtk,bhsk,bhtsk->bhts', qb, kb, decay)
        o = jnp.einsum('bhts,bhsv->bhtv', A, vb) + jnp.einsum('bhtk,bhkv->bhtv', qb * jnp.exp(b), S)
        bl = b[:, :, -1:, :]
        S = jnp.exp(bl[:, :, 0, :])[..., None] * S + jnp.einsum('bhsk,bhsv->bhkv', kb * jnp.exp(bl - b), vb)
        return S, o

    S, o = lax.scan(step, S0.astype(jnp.float32), (qc, kc, vc, gc))
    o = o.transpose(1, 0, 3, 2, 4).reshape(B, N * C, H, dv)[:, :T]
    return o, S

def softmax_rows(s, v, contract):
    m = jnp.max(s, axis=-1, keepdims=True)
    p = jnp.exp(s - m)
    den = jnp.sum(p, axis=-1, keepdims=True)
    o = jnp.einsum(contract, p, v.astype(jnp.float32)) / den
    return o, (m + jnp.log(den))[..., 0]

def dilated_window_prompt(q, k, v, dil, n_back):
    B, H, T, dh = q.shape
    L = T // dil
    nb = -(-L // ATT_BLOCK)
    Lp = nb * ATT_BLOCK

    def stream(a):
        a = a.reshape(B, H, L, dil, dh).transpose(0, 1, 3, 2, 4)
        a = jnp.pad(a, ((0, 0), (0, 0), (0, 0), (0, Lp - L), (0, 0)))
        return a.reshape(B, H, dil, nb, ATT_BLOCK, dh)

    def with_prev(a):
        prev = jnp.pad(a[:, :, :, :-1], ((0, 0), (0, 0), (0, 0), (1, 0), (0, 0), (0, 0)))
        return jnp.concatenate([prev, a], axis=4)

    qs = stream(q)
    k2, v2 = with_prev(stream(k)), with_prev(stream(v))
    s = jnp.einsum('bhrnqd,bhrnkd->bhrnqk', qs, k2, preferred_element_type=jnp.float32) * (HEAD_DIM ** -0.5)
    qi = jnp.arange(ATT_BLOCK)[:, None]
    ki = jnp.arange(2 * ATT_BLOCK)[None, :] - ATT_BLOCK
    rel = qi - ki
    kpos = jnp.arange(nb)[:, None, None] * ATT_BLOCK + ki[None]
    mask = (rel >= 0) & (rel <= n_back) & (kpos >= 0)
    s = jnp.where(mask, s, -jnp.inf)
    o, lse = softmax_rows(s, v2, 'bhrnqk,bhrnkd->bhrnqd')
    o = o.reshape(B, H, dil, Lp, dh)[:, :, :, :L].transpose(0, 1, 3, 2, 4).reshape(B, H, T, dh)
    lse = lse.reshape(B, H, dil, Lp)[..., :L].transpose(0, 1, 3, 2).reshape(B, H, T)
    return o, lse

def dilated_window_sample(q, k_all, v_all, dil, n_back, buf_len):
    T = q.shape[2]
    idx = buf_len + jnp.arange(T)[:, None] - jnp.arange(n_back + 1)[None, :] * dil
    valid = idx >= 0
    idx = jnp.maximum(idx, 0)
    kg, vg = k_all[:, :, idx], v_all[:, :, idx]
    s = jnp.einsum('bhtd,bhtnd->bhtn', q, kg, preferred_element_type=jnp.float32) * (HEAD_DIM ** -0.5)
    s = jnp.where(valid, s, -jnp.inf)
    return softmax_rows(s, vg, 'bhtn,bhtnd->bhtd')

def peer(n, wq, qn_w, k1, k2, u, v):
    B, T, D = n.shape
    flat = n.reshape(-1, D)
    N = flat.shape[0]
    blk = min(P_BLOCK, N)
    pad = (-N) % blk
    flat = jnp.pad(flat, ((0, pad), (0, 0)))

    def one_block(xb):
        q = rms_norm((xb @ wq).reshape(blk, P_HEADS, P_QDIM), qn_w)
        s1 = jnp.einsum('thd,hnd->thn', q[..., :P_HALF], k1, preferred_element_type=jnp.float32)
        s2 = jnp.einsum('thd,hnd->thn', q[..., P_HALF:], k2, preferred_element_type=jnp.float32)
        v1, i1 = lax.top_k(s1, P_TOPK)
        v2, i2 = lax.top_k(s2, P_TOPK)
        cand = (v1[..., :, None] + v2[..., None, :]).reshape(blk, P_HEADS, P_TOPK * P_TOPK)
        cidx = (i1[..., :, None] * N_KEYS + i2[..., None, :]).reshape(blk, P_HEADS, P_TOPK * P_TOPK)
        sc, sel = lax.top_k(cand, P_TOPK)
        eidx = jnp.take_along_axis(cidx, sel, axis=-1)
        g = jax.nn.softmax(sc, axis=-1)
        act = jax.nn.gelu(jnp.einsum('td,thkd->thk', xb, u[eidx], preferred_element_type=jnp.float32))
        return jnp.einsum('thk,thkd->td', (g * act).astype(xb.dtype), v[eidx])

    out = lax.map(one_block, flat.reshape(-1, blk, D)).reshape(-1, D)[:N]
    return out.reshape(B, T, D)

def decoder_layer(x, c, pos, lb, S0, kv_bufs, w_ada, b_ada, norm1_w, norm2_w, w_in, hgrn_norm_w,
                  q_norm_w, k_norm_w, w_branch_a, w_branch_b, w_out, peer_wq, peer_qn_w,
                  peer_k1, peer_k2, peer_u, peer_v):
    B, T, _ = x.shape
    mod = jax.nn.silu(c) @ w_ada + b_ada
    sh1, sc1, g1, sh2, sc2, g2 = jnp.split(mod[:, None, :], 6, axis=-1)
    n1 = rms_norm(x, norm1_w) * (1 + sc1) + sh1
    h = n1 @ w_in
    qa, fa, ia, ga, qb, kb, vb, gl = jnp.split(h, SPLITS, axis=-1)

    f = lb + (1 - lb) * jax.nn.sigmoid(fa.astype(jnp.float32))
    heads = lambda a: a.reshape(B, T, A_HEADS, -1)
    oa, S_new = hgrn_chunked(heads(qa), heads(1 - f), heads(ia), heads(jnp.log(f)), S0)
    oa = rms_norm(oa.astype(x.dtype), hgrn_norm_w) * jax.nn.silu(heads(ga))
    ya = oa.reshape(B, T, A_WIDTH) @ w_branch_a

    att_heads = lambda a: a.reshape(B, T, N_GROUPS * G_HEADS, HEAD_DIM).transpose(0, 2, 1, 3)
    q = partial_rope(rms_norm(att_heads(qb), q_norm_w), pos)
    k = partial_rope(rms_norm(att_heads(kb), k_norm_w), pos)
    v = att_heads(vb)
    outs, lses, new_kv = [], [], []
    for gi, (win, dil) in enumerate(ATT_GROUPS):
        sl = slice(gi * G_HEADS, (gi + 1) * G_HEADS)
        qg, kg, vg = q[:, sl], k[:, sl], v[:, sl]
        n_back = win // dil
        if kv_bufs is None:
            o, lse = dilated_window_prompt(qg, kg, vg, dil, n_back)
            keep = min(win, T)
            new_kv.append(jnp.stack([kg[:, :, T - keep:], vg[:, :, T - keep:]], axis=1))
        else:
            buf = kv_bufs[gi]
            o, lse = dilated_window_sample(qg, jnp.concatenate([buf[:, 0], kg], axis=2),
                                           jnp.concatenate([buf[:, 1], vg], axis=2),
                                           dil, n_back, buf.shape[3])
            new_kv.append(jnp.stack([kg, vg], axis=1))
        outs.append(o)
        lses.append(lse)
    wts = jax.nn.softmax(jnp.stack(lses), axis=0)
    ob = jnp.sum(wts[..., None] * jnp.stack(outs), axis=0)
    yb = ob.transpose(0, 2, 1, 3).reshape(B, T, G_HEADS * HEAD_DIM).astype(x.dtype) @ w_branch_b

    gate_a, gate_b = jnp.split(jax.nn.sigmoid(gl), 2, axis=-1)
    x = x + g1 * ((gate_a * ya + gate_b * yb) @ w_out)

    n2 = rms_norm(x, norm2_w) * (1 + sc2) + sh2
    x = x + g2 * peer(n2, peer_wq, peer_qn_w, peer_k1, peer_k2, peer_u, peer_v)
    return x, new_kv, S_new

def setup_inputs(seed: int = 0) -> dict:
    key = jax.random.key(seed)
    ks = iter(jax.random.split(key, 32))
    nrm = lambda shape, scale: jax.random.normal(next(ks), shape, jnp.float32) * scale
    gain = lambda shape: 1.0 + nrm(shape, 0.02)
    D = D_MODEL
    return {
        "x_prompt": nrm((BATCH, SEQ, D), 1.0),
        "x_sample": nrm((DEC_BATCH, DEC_SEQ, D), 1.0),
        "cache_kv_g1": nrm((DEPTH, DEC_BATCH, 2, G_HEADS, min(ATT_GROUPS[0][0], PAST_LEN), HEAD_DIM), 1.0),
        "cache_kv_g2": nrm((DEPTH, DEC_BATCH, 2, G_HEADS, min(ATT_GROUPS[1][0], PAST_LEN), HEAD_DIM), 1.0),
        "cache_kv_g3": nrm((DEPTH, DEC_BATCH, 2, G_HEADS, min(ATT_GROUPS[2][0], PAST_LEN), HEAD_DIM), 1.0),
        "state_hgrn": nrm((DEPTH, DEC_BATCH, A_HEADS, A_DK, A_DV), 1.0),
        "c_prompt": nrm((BATCH, D), 1.0),
        "c_sample": nrm((DEC_BATCH, D), 1.0),
        "w_ada": nrm((DEPTH, D, 6 * D), 0.5 * D ** -0.5),
        "b_ada": nrm((DEPTH, 6 * D), 0.02),
        "norm1_w": gain((DEPTH, D)),
        "norm2_w": gain((DEPTH, D)),
        "w_in": nrm((DEPTH, D, IN_COLS), D ** -0.5),
        "lb_logits": nrm((DEPTH + 1, A_WIDTH), 0.5),
        "hgrn_norm_w": gain((DEPTH, A_DV)),
        "q_norm_w": gain((DEPTH, HEAD_DIM)),
        "k_norm_w": gain((DEPTH, HEAD_DIM)),
        "w_branch_a": nrm((DEPTH, A_WIDTH, D), A_WIDTH ** -0.5),
        "w_branch_b": nrm((DEPTH, G_HEADS * HEAD_DIM, D), (G_HEADS * HEAD_DIM) ** -0.5),
        "w_out": nrm((DEPTH, D, D), D ** -0.5),
        "peer_wq": nrm((DEPTH, D, P_HEADS * P_QDIM), D ** -0.5),
        "peer_qn_w": gain((DEPTH, P_QDIM)),
        "peer_k1": nrm((DEPTH, P_HEADS, N_KEYS, P_HALF), P_HALF ** -0.5),
        "peer_k2": nrm((DEPTH, P_HEADS, N_KEYS, P_HALF), P_HALF ** -0.5),
        "peer_u": nrm((DEPTH, N_EXPERTS, D), D ** -0.5),
        "peer_v": nrm((DEPTH, N_EXPERTS, D), P_HEADS ** -0.5),
    }

def reference(x_prompt, x_sample, cache_kv_g1, cache_kv_g2, cache_kv_g3, state_hgrn, c_prompt, c_sample,
              w_ada, b_ada, norm1_w, norm2_w, w_in, lb_logits, hgrn_norm_w, q_norm_w, k_norm_w,
              w_branch_a, w_branch_b, w_out, peer_wq, peer_qn_w, peer_k1, peer_k2, peer_u, peer_v):
    pos_p = jnp.arange(x_prompt.shape[1])
    pos_s = PAST_LEN + jnp.arange(x_sample.shape[1])
    lb_all = jnp.cumsum(jax.nn.softmax(lb_logits.astype(jnp.float32), axis=0), axis=0)
    yp, ys = x_prompt, x_sample
    kvp = ([], [], [])
    kvs = ([], [], [])
    Sp_list, Ss_list = [], []
    for l in range(DEPTH):
        wl = (w_ada[l], b_ada[l], norm1_w[l], norm2_w[l], w_in[l], hgrn_norm_w[l], q_norm_w[l], k_norm_w[l],
              w_branch_a[l], w_branch_b[l], w_out[l], peer_wq[l], peer_qn_w[l], peer_k1[l], peer_k2[l],
              peer_u[l], peer_v[l])
        S0p = jnp.zeros((yp.shape[0], A_HEADS, A_DK, A_DV), jnp.float32)
        yp, nkv_p, Sp = decoder_layer(yp, c_prompt, pos_p, lb_all[l], S0p, None, *wl)
        ys, nkv_s, Ss = decoder_layer(ys, c_sample, pos_s, lb_all[l], state_hgrn[l],
                                      (cache_kv_g1[l], cache_kv_g2[l], cache_kv_g3[l]), *wl)
        for gi in range(N_GROUPS):
            kvp[gi].append(nkv_p[gi])
            kvs[gi].append(nkv_s[gi])
        Sp_list.append(Sp.astype(yp.dtype))
        Ss_list.append(Ss.astype(state_hgrn.dtype))
    new_kv_g1_prompt = jnp.stack(kvp[0])
    new_kv_g2_prompt = jnp.stack(kvp[1])
    new_kv_g3_prompt = jnp.stack(kvp[2])
    new_state_hgrn_prompt = jnp.stack(Sp_list)
    new_kv_g1_sample = jnp.stack(kvs[0])
    new_kv_g2_sample = jnp.stack(kvs[1])
    new_kv_g3_sample = jnp.stack(kvs[2])
    new_state_hgrn_sample = jnp.stack(Ss_list)
    return (yp, ys, new_kv_g1_prompt, new_kv_g2_prompt, new_kv_g3_prompt, new_state_hgrn_prompt,
            new_kv_g1_sample, new_kv_g2_sample, new_kv_g3_sample, new_state_hgrn_sample)


_drawn_inputs = setup_inputs


def setup_inputs(seed=0):
    import zlib

    import numpy as np

    out = dict(_drawn_inputs(seed))
    spreads = {}
    factors = {'cache_kv_g1': 5.8,
     'cache_kv_g2': 5.959,
     'cache_kv_g3': 6.173,
     'norm1_w': 3.011,
     'norm2_w': 20.1,
     'hgrn_norm_w': 8.0,
     'q_norm_w': 8.0,
     'k_norm_w': 4.031,
     'peer_qn_w': 22.854}
    for name, (base, spread) in spreads.items():
        noise = np.random.default_rng([zlib.crc32(name.encode()), seed]).standard_normal(out[name].shape)
        drawn = base * np.exp(spread * noise) if base else spread * noise
        out[name] = __import__('jax').numpy.asarray(drawn.astype(out[name].dtype))
    for name, factor in factors.items():
        out[name] = (out[name] * factor).astype(out[name].dtype)
    return out
```

```python
import numpy as np
import concourse.bass as bass
from concourse import mybir
from contextlib import ExitStack

F32 = mybir.dt.float32
F32R = mybir.dt.float32r
U32 = mybir.dt.uint32
I32 = mybir.dt.int32
ALU = mybir.AluOpType
ACT = mybir.ActivationFunctionType
AX_X = mybir.AxisListType.X

P = 128
D = 1024
DC = D // P
SEQ = 1024
DEC_B, DEC_T, PAST = 8, 4, 2048
S_TOK = DEC_B * DEC_T
TOK = SEQ + S_TOK
N_TILES = SEQ // P + 1
HEADS, DH = 4, 128
WIDTH = HEADS * DH
GROUPS = ((128, 1), (512, 4), (2048, 16))
ROT = DH // 4
HALF_ROT = ROT // 2
THETA = 500000.0
CHUNK = 32
N_CH = P // CHUNK
PH, TOPK, N_KEYS = 8, 16, 128
RING = 8
EPS = 1e-6
LOWEST = -3.0e38
MASKED = -1.0e30
START = 1
BLOCK = 512

T_Q, T_F, T_G, T_GATE = 0, WIDTH, 2 * WIDTH, 3 * WIDTH
R_I, R_Q, R_K, R_V = 0, WIDTH, 4 * WIDTH, 7 * WIDTH


class Order:

    def __init__(self, eng, sem):
        self.eng, self.sem, self.n = eng, sem, 0

    def link(self, ins):
        self.n += 1
        ins.then_inc(self.sem, 1)
        self.eng.wait_ge(self.sem, self.n)

    def restart(self):
        if self.n:
            self.eng.sem_clear(self.sem)
        self.n = 0


def wait_apart(eng, sem, value, done_sem, done_value):
    if not isinstance(value, int):
        value = eng.to_reg(value)
    eng.wait_ge(done_sem, done_value)
    eng.wait_ge(sem, value)


def consts_phase(nc, sem, const):
    block_ready = sem("const_parts")
    with nc.Block() as block:
        @block.gpsimd
        def _(pool):
            nc.gpsimd.memset(const["zeros"][:], 0.0)
            nc.gpsimd.memset(const["ones"][:], 1.0)
            nc.gpsimd.memset(const["eps"][:], EPS)
            nc.gpsimd.memset(const["ident"][:], 0.0).then_inc(block_ready, 1)
            pool.wait_ge(block_ready, 1)
            nc.gpsimd.affine_select(out=const["ident"][:], in_=const["ident"][:], compare_op=ALU.not_equal,
                                    fill=1.0, base=0, pattern=[[-1, P]], channel_multiplier=1)
            nc.gpsimd.iota(const["iota16"][:], pattern=[[1, TOPK]], base=0, channel_multiplier=0,
                           allow_small_or_imprecise_dtypes=True).then_inc(const["ready"], 3)


def mod_phase(nc, ctx, sem, const, x, dram):
    sb = lambda name, shape, dt=F32: ctx.enter_context(nc.sbuf_tensor(name, shape, dt))
    psum = lambda name, shape: ctx.enter_context(nc.psum_tensor(name, shape, F32))
    R = 1 + DEC_B
    N_BLOCKS = 6 * D // BLOCK
    c_rows = sb("c_rows", [R, D])
    silu_c = sb("silu_c", [R, D])
    c_t = sb("c_t", [P, DC, R])
    bias = sb("ada_bias", [R, 6 * D])
    w = sb("ada_w", [P, 2, DC, BLOCK])
    out = sb("mod_rows", [R, 2, BLOCK])
    c_psum = psum("c_psum", [P, DC, R])
    acc = psum("mod_acc", [R, 2, BLOCK])
    c_loaded, silu_done, c_turned, c_copied = sem("c_loaded"), sem("silu_done"), sem("c_turned"), sem("c_copied")
    w_loaded = [sem("ada_w0_loaded"), sem("ada_w1_loaded")]
    product_done, row_ready = sem("mod_product_done"), sem("mod_row_ready", START)
    stored = [sem("mod0_stored", START), sem("mod1_stored", START)]
    w_dram = x["w_ada"][0].rearrange("(c p) n -> p c n", p=P)
    block = ctx.enter_context(nc.Block())

    @block.sync
    def _(sp):
        sp.dma_start(c_rows[0:1, :], x["c_prompt"]).then_inc(c_loaded, 16)
        sp.dma_start(c_rows[1:R, :], x["c_sample"]).then_inc(c_loaded, 16)
        sp.dma_start(bias[:], x["b_ada"][0:1, :].broadcast_to([R, 6 * D])).then_inc(c_loaded, 16)
        for s in range(2):
            sp.dma_start(w[:, s], w_dram[:, :, s * BLOCK:(s + 1) * BLOCK]).then_inc(w_loaded[s], 16)
        with sp.Fori(1, N_BLOCKS // 2) as i:
            for s in range(2):
                sp.wait_ge(product_done, 2 * i + s - 1)
                sp.dma_start(w[:, s], w_dram[:, :, bass.ds((2 * i + s) * BLOCK, BLOCK)]).then_inc(w_loaded[s], 16)

    @block.scalar
    def _(act):
        act.wait_ge(c_loaded, 48)
        nc.scalar.activation(silu_c[:], c_rows[:], ACT.Silu).then_inc(silu_done, 1)
        with act.Fori(0, N_BLOCKS // 2) as i:
            for s in range(2):
                act.wait_ge(row_ready, 2 * i + s + 1 + START)
                act.dma_start(dram["mod"][:, bass.ds((2 * i + s) * BLOCK, BLOCK)], out[:, s, :]).then_inc(stored[s], 16)
        for s in range(2):
            act.wait_ge(stored[s], 16 * (N_BLOCKS // 2) + START)

    @block.tensor
    def _(pe):
        pe.wait_ge(silu_done, 1)
        for c in range(DC):
            ins = nc.tensor.transpose(c_psum[:, c, :], silu_c[:, c * P:(c + 1) * P], const["ident"][0:R, 0:R])
        ins.then_inc(c_turned, 1)
        pe.wait_ge(c_copied, 1)
        with pe.Fori(0, N_BLOCKS // 2) as i:
            for s in range(2):
                pe.wait_ge(w_loaded[s], 16 * i + 16)
                wait_apart(pe, row_ready, ((2 * i + s) - 1 if s else 2 * i) + START, c_copied, 1)
                for c in range(DC):
                    ins = nc.tensor.matmul(acc[:, s, :], c_t[:, c, :], w[:, s, c, :], start=(c == 0), stop=(c == DC - 1))
                ins.then_inc(product_done, 1)

    @block.vector
    def _(dve):
        dve.wait_ge(c_turned, 1)
        nc.vector.tensor_copy(c_t[:], c_psum[:]).then_inc(c_copied, 1)
        with dve.Fori(0, N_BLOCKS // 2) as i:
            for s in range(2):
                dve.wait_ge(product_done, 2 * i + s + 1)
                dve.wait_ge(stored[s], 16 * i + START)
                nc.vector.tensor_tensor(out[:, s, :], acc[:, s, :], bias[:, bass.ds((2 * i + s) * BLOCK, BLOCK)],
                                        ALU.add).then_inc(row_ready, 1)


def norm_phase(nc, ctx, sem, const, tag, src_rows, norm_w, mod, shift_at, scale_at, n_hi, n_lo, keep_rows):
    sb = lambda name, shape, dt=F32: ctx.enter_context(nc.sbuf_tensor(name + tag, shape, dt))
    rows = sb("norm_rows", [P, 2, D])
    normed = sb("normed", [P, 2, D])
    junk = sb("norm_junk", [P, D])
    stat = sb("norm_stat", [P, 2, 3])
    scale_p, shift_p = sb("scale_p", [P, D]), sb("shift_p", [P, D])
    scale_s, shift_s = sb("scale_s", [S_TOK, D]), sb("shift_s", [S_TOK, D])
    weight = sb("norm_weight", [P, D])
    mark = sb("norm_mark", [1, 1])
    turned = ctx.enter_context(nc.psum_tensor("turned" + tag, [P, 2, DC, P], F32))
    s_ = lambda name, start=0: sem(name + tag, start)
    mod_loaded, own, gains_ready = s_("mod_loaded"), s_("norm_own"), s_("gains_ready")
    rows_loaded = [s_("rows0_loaded"), s_("rows1_loaded")]
    squares_done, root_done, rstd_ready, normed_ready = s_("squares_done"), s_("root_done"), s_("rstd_ready"), s_("normed_ready", START)
    turned_done, copied = s_("turned_done"), s_("n_t_copied")
    kept = [s_("kept0", START), s_("kept1", START)]
    N_PAIRS = (N_TILES - 1) // 2
    block = ctx.enter_context(nc.Block())

    def all_tiles(eng, run):
        with eng.Fori(0, N_PAIRS) as i:
            for s in range(2):
                run(i * 2 + s, i, s, P)
        run(N_TILES - 1, N_PAIRS, 0, S_TOK)

    @block.sync
    def _(sp):
        sp.dma_start(weight[:], norm_w.broadcast_to([P, D])).then_inc(mod_loaded, 16)
        sp.dma_start(scale_p[:], mod[0:1, scale_at:scale_at + D].broadcast_to([P, D])).then_inc(mod_loaded, 16)
        sp.dma_start(shift_p[:], mod[0:1, shift_at:shift_at + D].broadcast_to([P, D])).then_inc(mod_loaded, 16)
        for b in range(DEC_B):
            t = slice(b * DEC_T, (b + 1) * DEC_T)
            sp.dma_start(scale_s[t, :], mod[b + 1:b + 2, scale_at:scale_at + D].broadcast_to([DEC_T, D])).then_inc(mod_loaded, 16)
            sp.dma_start(shift_s[t, :], mod[b + 1:b + 2, shift_at:shift_at + D].broadcast_to([DEC_T, D])).then_inc(mod_loaded, 16)

        def run(n, i, s, w):
            sp.wait_ge(normed_ready, n + START)
            sp.dma_start(rows[0:w, s, :], src_rows(n, w)).then_inc(rows_loaded[s], 16)

        all_tiles(sp, run)

    @block.scalar
    def _(act):
        own_order = Order(act, own)

        def run(n, i, s, w):
            act.wait_ge(rows_loaded[s], 16 * i + 16)
            own_order.link(nc.scalar.activation(junk[0:w, :], rows[0:w, s, :], ACT.Square, accum_out=stat[0:w, s, 0:1]))
            nc.scalar.activation(stat[0:w, s, 1:2], stat[0:w, s, 0:1], ACT.Sqrt, bias=const["eps"][0:w, :],
                                 scale=1.0 / D).then_inc(root_done, 1)
            if keep_rows is not None:
                act.wait_ge(normed_ready, n + 2 + START)
                act.dma_start(keep_rows(n, w), normed[0:w, s, :]).then_inc(kept[s], 16)
            own_order.restart()

        all_tiles(act, run)
        if keep_rows is not None:
            act.wait_ge(kept[0], 16 * (N_PAIRS + 1) + START)
            act.wait_ge(kept[1], 16 * N_PAIRS + START)

    @block.vector
    def _(dve):
        order = Order(dve, rstd_ready)
        dve.wait_ge(mod_loaded, 16 * (3 + 2 * DEC_B))
        order.link(nc.vector.tensor_scalar(scale_p[:], scale_p[:], 1.0, None, ALU.add))
        order.link(nc.vector.tensor_tensor(scale_p[:], scale_p[:], weight[:], ALU.mult))
        order.link(nc.vector.tensor_scalar(scale_s[:], scale_s[:], 1.0, None, ALU.add))
        order.link(nc.vector.tensor_tensor(scale_s[:], scale_s[:], weight[0:S_TOK, :], ALU.mult))
        order.restart()
        nc.vector.memset(mark[:], 0.0).then_inc(normed_ready, 1)

        def run(n, i, s, w):
            gain, shift = (scale_p, shift_p) if w == P else (scale_s, shift_s)
            dve.wait_ge(root_done, n + 1)
            order.link(nc.vector.reciprocal(stat[0:w, s, 2:3], stat[0:w, s, 1:2]))
            if keep_rows is not None:
                dve.wait_ge(kept[s], 16 * i + START)
            order.link(nc.vector.scalar_tensor_tensor(out=normed[0:w, s, :], in0=rows[0:w, s, :], scalar=stat[0:w, s, 2:3],
                                                      in1=gain[0:w, :], op0=ALU.mult, op1=ALU.mult))
            nc.vector.tensor_tensor(normed[0:w, s, :], normed[0:w, s, :], shift[0:w, :], ALU.add).then_inc(normed_ready, 1)
            dve.wait_ge(turned_done, n + 1)
            part = (slice(None), slice(None), bass.ds(n * P, w))
            order.link(nc.vector.tensor_copy(n_hi[part], turned[:, s, :, 0:w]))
            nc.vector.tensor_tensor(n_lo[part], turned[:, s, :, 0:w], n_hi[part].bitcast(F32), ALU.subtract).then_inc(copied, 1)
            order.restart()

        all_tiles(dve, run)

    @block.tensor
    def _(pe):
        def run(n, i, s, w):
            pe.wait_ge(normed_ready, n + 2 + START)
            for c in range(DC):
                ins = nc.tensor.transpose(turned[:, s, c, 0:w], normed[0:w, s, c * P:(c + 1) * P], const["ident"][0:w, 0:w])
            ins.then_inc(turned_done, 1)

        all_tiles(pe, run)


def project_phase(nc, ctx, sem, const, n_hi, n_lo, x, consts, dram, new_state_p, new_state_s):
    sb = lambda name, shape, dt=F32: ctx.enter_context(nc.sbuf_tensor(name, shape, dt))
    psum = lambda name, shape: ctx.enter_context(nc.psum_tensor(name, shape, F32))
    f_raw = sb("f_raw", [P, 2, HEADS, P])
    q_in = sb("q_in", [P, 2, HEADS, P])
    g_in = sb("g_in", [P, 2, HEADS, P])
    v_in = sb("v_in", [P, 2, WIDTH])
    forget = sb("forget", [P, HEADS, P])
    key = sb("key", [P, HEADS, P])
    logf = sb("logf", [P, HEADS, P])
    cum = sb("cum", [P, HEADS, P])
    cum_mid = sb("cum_mid", [P, HEADS, P])
    cum_end = sb("cum_end", [P, HEADS, P])
    e_k = sb("e_k", [P, HEADS, P])
    e_q, e_in, e_out = cum_mid, cum, cum_end
    decay = sb("decay", [P, HEADS * DEC_B])
    k_rows = sb("k_rows", [P, HEADS, P])
    attn = sb("attn", [P, HEADS, CHUNK])
    attn_s = sb("attn_s", [S_TOK, HEADS, S_TOK])
    v_one = [a[0:S_TOK].rearrange("p h t -> p (h t)") for a in (e_k, logf)]
    state = sb("state", [P, 2, HEADS, P])
    state_in = sb("state_in", [P, DEC_B, HEADS, P])
    state_out = sb("state_out", [P, 2, HEADS, P])
    square, root, rstd = key, forget, forget
    normed = sb("o_normed", [P, 2, HEADS, P])
    reset = sb("chunk_reset", [P, P])
    reset_s = sb("chunk_reset_s", [P, S_TOK])
    causal = sb("chunk_causal", [P, HEADS, CHUNK], I32)
    causal_s = sb("sample_causal", [S_TOK, HEADS, S_TOK], I32)
    own_row = sb("own_row", [S_TOK, DEC_B])
    lb_pair = sb("lb_pair", [P, 2, HEADS])
    lb_max, lb_sum = sb("lb_max", [P, HEADS]), sb("lb_sum", [P, HEADS])
    lb, lb_rest = sb("lb", [P, HEADS]), sb("lb_rest", [P, HEADS])
    head_w = sb("head_w", [P, 1])
    turned = psum("k_turned", [P, HEADS, P])
    sums = turned
    scores = psum("a_scores", [P, BLOCK])
    update = psum("state_update", [P, 2, WIDTH])
    out = psum("o_out", [P, HEADS, P])
    SLOTS = 3
    W_PART = 2
    w_part = sb("in_w", [P, W_PART, BLOCK])
    w_hi, w_lo = sb("in_w_hi", [P, 2, DC, BLOCK], F32R), sb("in_w_lo", [P, 2, DC, BLOCK], F32R)
    w_split = sem("in_w_split")
    split_own = sem("split_own")
    stage = sb("h_stage", [P, SLOTS, BLOCK])
    acc = psum("h_acc", [P, SLOTS, BLOCK])
    w_loaded = sem("in_w_loaded")
    unit_done, unit_copied = sem("h_unit_done"), sem("h_unit_copied")
    h_stored = [sem(f"h_stored{k}") for k in range(SLOTS)]

    consts_in = sem("hgrn_consts_loaded")
    loaded = [sem("hgrn_in0"), sem("hgrn_in1")]
    sig_done, f_done, log_done, cum_done, exps_done = sem("sig_done"), sem("f_done"), sem("log_done"), sem("cum_done"), sem("exps_done")
    scaled_done, pe_turned, rows_copied, updates_done = sem("scaled_done"), sem("k_turned_done"), sem("k_rows_copied"), sem("updates_done")
    chunk_done, state_done, squares, sums_done, roots_done = sem("o_chunk_done", START), sem("state_done", START), sem("o_squares"), sem("o_sums_done"), sem("o_roots_done")
    normed_done, lb_shifted, lb_exps, s_in, s_row = sem("o_normed_done", START), sem("lb_shifted"), sem("lb_exps"), sem("s_state_in"), sem("s_row_ready")
    oa_stored = sem("oa_stored")
    oa_out = sem("oa_out", START + 1)
    state_stored = [sem("state_stored0"), sem("state_stored1")]
    final_stored = sem("p_state_stored")
    dve_own, act_own = sem("hgrn_dve_own"), sem("hgrn_act_own")
    update_s = sem("s_update_done")
    N_PAIRS = SEQ // P // 2
    N_P = SEQ // P
    T_UNITS = [(m, t0, n) for m in range(BLOCK // P) for t0, n in ((0, 512), (512, 512), (SEQ, S_TOK))]
    R_UNITS = [(t, P if t < N_TILES - 1 else S_TOK) for t in range(N_TILES)]
    units_of = lambda kind: T_UNITS if kind == "T" else R_UNITS
    FIRST = [(0, "T", 0, None), (1, "T", 1, None), (2, "R", 0, None), (3, "T", 2, None)]
    LOOP_FROM = len(FIRST)
    LAST = [(12, "R", 9, "sample"), (13, "T", 3, "sample states"), (14, "T", 4, None), (15, "T", 5, None), (16, "T", 6, None)]
    assert LOOP_FROM % 2 == 0 and N_P % 2 == 0
    N_BLOCKS = LOOP_FROM + N_P + len(LAST)
    w_dram = x["w_in"][0].rearrange("(c p) n -> p c n", p=P)
    block = ctx.enter_context(nc.Block())

    def all_blocks(eng, run):
        before = 0
        for n, (_, kind, to, beside) in enumerate(FIRST):
            run(n, n % 2, n // 2, kind, to, before, before // SLOTS, beside)
            before += len(units_of(kind))
        r = len(R_UNITS)
        with eng.Fori(0, N_PAIRS) as i:
            for s in range(2):
                units = before + s * r
                run(i * 2 + (LOOP_FROM + s), s, i + LOOP_FROM // 2, "R", i * 2 + (1 + s), i * (2 * r) + units,
                    i * (2 * r // SLOTS) + units // SLOTS, (i * 2 + s, i, s))
        before += N_P * r
        for n, (_, kind, to, beside) in enumerate(LAST, LOOP_FROM + N_P):
            run(n, n % 2, n // 2, kind, to, before, before // SLOTS, beside)
            before += len(units_of(kind))
        return before

    def all_tiles(eng, run):
        with eng.Fori(0, N_PAIRS) as i:
            for s in range(2):
                run(i * 2 + s, i, s)

    h_t = lambda at, cols: dram["h_t"][at:at + WIDTH, cols].rearrange("(h p) t -> p h t", p=P)
    oa_t = lambda cols: dram["oa_t"][:, cols].rearrange("(h p) t -> p h t", p=P)
    lb_dram = x["lb_logits"].rearrange("l (h p) -> p l h", p=P)
    s_cols = slice(SEQ, TOK)
    st_dram = x["state_hgrn"][0].rearrange("b h k v -> k (b h) v")
    st_out = new_state_s[0].rearrange("b h k v -> k (b h) v")

    @block.sync
    def _(sp):
        def load_tile(cols, n, s):
            sp.dma_start(f_raw[:, s, :, 0:n], h_t(T_F, cols)).then_inc(loaded[s], 16)
            sp.dma_start(q_in[:, s, :, 0:n], h_t(T_Q, cols)).then_inc(loaded[s], 16)
            sp.dma_start(g_in[:, s, :, 0:n], h_t(T_G, cols)).then_inc(loaded[s], 16)
            sp.dma_start(v_in[0:n, s, :], dram["h_r"][cols, R_I:R_I + WIDTH]).then_inc(loaded[s], 16)

        sp.dma_start(reset[:], consts["chunk_reset"]).then_inc(consts_in, 16)
        sp.dma_start(reset_s[:], consts["chunk_reset_s"]).then_inc(consts_in, 16)
        sp.dma_start(causal[:].rearrange("p a b -> p (a b)"), consts["chunk_causal"]).then_inc(consts_in, 16)
        sp.dma_start(causal_s[:].rearrange("p a b -> p (a b)"), consts["sample_causal"]).then_inc(consts_in, 16)
        sp.dma_start(own_row[:], consts["own_row"]).then_inc(consts_in, 16)
        with nc.allow_non_contiguous_dma("one bound for each key column"):
            for l in range(2):
                sp.dma_start(lb_pair[:, l, :], lb_dram[:, l, :]).then_inc(consts_in, 16)
            sp.dma_start(head_w[:], x["hgrn_norm_w"].rearrange("a d -> d a")).then_inc(consts_in, 16)
        sp.dma_start(state_in[:].rearrange("p b h v -> p (b h) v"), st_dram).then_inc(s_in, 16)

        def run(n, s, w_round, kind, to, before, thirds, beside):
            if beside is not None and beside != "sample states":
                if isinstance(beside, tuple):
                    tile, tile_round, slot = beside
                    sp.wait_ge(normed_done, tile + START)
                    load_tile(bass.ds(tile * P, P), P, slot)
                else:
                    sp.wait_ge(normed_done, N_P + START)
                    load_tile(s_cols, S_TOK, 0)
            for u, unit in enumerate(units_of(kind)):
                sp.wait_ge(unit_copied, before + (u + 1))
                if kind == "T":
                    m, t0, k = unit
                    sp.dma_start(dram["h_t"][to * BLOCK + m * P:to * BLOCK + (m + 1) * P, t0:t0 + k],
                                 stage[:, u % SLOTS, 0:k]).then_inc(h_stored[u % SLOTS], 16)
                else:
                    t, k = unit
                    sp.dma_start(dram["h_r"][t * P:t * P + k, bass.ds(to * BLOCK, BLOCK)],
                                 stage[0:k, u % SLOTS, :]).then_inc(h_stored[u % SLOTS], 16)
            if isinstance(n, int) and n == LOOP_FROM - 1:
                for k in range(SLOTS):
                    sp.wait_ge(h_stored[k], 16 * ((before + len(units_of(kind))) // SLOTS))

        total = all_blocks(sp, run)
        for k in range(SLOTS):
            sp.wait_ge(h_stored[k], 16 * (total // SLOTS))

    @block.gpsimd
    def _(pool):
        def store(n, s, n_cols, cols):
            pool.wait_ge(normed_done, n + 2 + START)
            pool.dma_start(oa_t(cols), normed[:, s, :, 0:n_cols]).then_inc(oa_stored, 16)
            pool.wait_ge(oa_stored, n * 16 + 16)
            pool.sem_inc(oa_out, 1)

        def split(n, s):
            for k in range(DC // W_PART):
                c = slice(k * W_PART, (k + 1) * W_PART)
                pool.dma_start(w_part[:], w_dram[:, c, bass.ds(n * BLOCK, BLOCK)]).then_inc(w_loaded, 16)
                wait_apart(pool, w_loaded, n * (16 * DC // W_PART) + 16 * (k + 1), const["ready"], 3)
                nc.gpsimd.tensor_copy(w_hi[:, s, c], w_part[:]).then_inc(split_own, 1)
                pool.wait_ge(split_own, 1)
                nc.gpsimd.tensor_tensor(w_lo[:, s, c], w_part[:], w_hi[:, s, c].bitcast(F32), ALU.subtract).then_inc(split_own, 1)
                pool.wait_ge(split_own, 2)
                pool.sem_clear(split_own)
            pool.sem_inc(w_split, 1)

        def run(n, s, w_round, kind, to, before, thirds, beside):
            if not (isinstance(n, int) and n == N_BLOCKS - 1):
                if not (isinstance(n, int) and n == 0):
                    wait_apart(pool, unit_done, before, const["ready"], 3)
                split(n + 1, 1 - s)
            if isinstance(beside, tuple):
                tile, tile_round, slot = beside
                store(tile, slot, P, bass.ds(tile * P, P))
            elif beside == "sample":
                pool.dma_start(new_state_p[0, 0].rearrange("h k v -> k h v"), state[:, 0]).then_inc(final_stored, 16)
            elif beside == "sample states":
                for b in range(DEC_B):
                    pool.wait_ge(s_row, b + 1)
                    pool.dma_start(st_out[:, b * HEADS:(b + 1) * HEADS, :], state_out[:, b % 2]).then_inc(state_stored[b % 2], 16)
                store(N_P, 0, S_TOK, s_cols)

        split(0, 0)
        all_blocks(pool, run)
        pool.wait_ge(state_stored[0], 16 * DEC_B // 2)
        pool.wait_ge(state_stored[1], 16 * DEC_B // 2)
        pool.wait_ge(final_stored, 16)

    @block.scalar
    def _(act):
        order = Order(act, act_own)
        act.wait_ge(lb_shifted, 1)
        nc.scalar.activation(lb_pair[:], lb_pair[:], ACT.Exp).then_inc(lb_exps, 1)

        def gates(n, tile_round, s, n_cols):
            act.wait_ge(loaded[s], tile_round * 64 + 64)
            act.wait_ge(normed_done, n + 1 + START)
            order.link(nc.scalar.activation(g_in[:, s, :, 0:n_cols], g_in[:, s, :, 0:n_cols], ACT.Silu))
            nc.scalar.activation(forget[:, :, 0:n_cols], f_raw[:, s, :, 0:n_cols], ACT.Sigmoid).then_inc(sig_done, 1)
            act.wait_ge(f_done, n + 1)
            nc.scalar.activation(logf[:, :, 0:n_cols], forget[:, :, 0:n_cols], ACT.Ln).then_inc(log_done, 1)

        def decays(n, n_cols):
            act.wait_ge(cum_done, n + 1)
            nc.scalar.activation(e_k[:, :, 0:n_cols], cum_mid[:, :, 0:n_cols], ACT.Exp, scale=-1.0)
            nc.scalar.activation(e_q[:, :, 0:n_cols], cum_mid[:, :, 0:n_cols], ACT.Exp)
            nc.scalar.activation(e_in[:, :, 0:n_cols], cum[:, :, 0:n_cols], ACT.Exp)
            nc.scalar.activation(e_out[:, :, 0:n_cols], cum_end[:, :, 0:n_cols], ACT.Exp).then_inc(exps_done, 1)

        def squared(n, n_cols):
            act.wait_ge(chunk_done, (n + 1) * N_CH + START)
            nc.scalar.activation(square[:, :, 0:n_cols], out[:, :, 0:n_cols], ACT.Square).then_inc(squares, 1)

        def roots(n, n_cols):
            act.wait_ge(sums_done, n + 1)
            nc.scalar.activation(root[:, :, 0:n_cols], sums[:, :, 0:n_cols], ACT.Sqrt, bias=const["eps"][:, :],
                                 scale=1.0 / DH).then_inc(roots_done, 1)

        def run(n, s, w_round, kind, to, before, thirds, beside):
            after = {}
            if isinstance(beside, tuple):
                tile, tile_round, slot = beside
                gates(tile, tile_round, slot, P)
                after = {0: lambda: decays(tile, P), 7: lambda: squared(tile, P),
                         8: lambda: roots(tile, P)}
            elif beside == "sample":
                gates(N_P, N_PAIRS, 0, S_TOK)
                after = {0: lambda: decays(N_P, S_TOK), 5: lambda: squared(N_P, S_TOK),
                         6: lambda: roots(N_P, S_TOK)}
            for u, unit in enumerate(units_of(kind)):
                p, k = (P, unit[2]) if kind == "T" else (unit[1], BLOCK)
                act.wait_ge(unit_done, before + (u + 1))
                if not (isinstance(before, int) and before + u < SLOTS):
                    act.wait_ge(h_stored[u % SLOTS], (thirds + u // SLOTS) * 16)
                nc.scalar.copy(stage[0:p, u % SLOTS, 0:k], acc[0:p, u % SLOTS, 0:k]).then_inc(unit_copied, 1)
                if u in after:
                    after[u]()
            order.restart()

        all_blocks(act, run)

    @block.vector
    def _(dve):
        order = Order(dve, dve_own)
        link = order.link
        nc.vector.memset(attn[:], 0.0)
        nc.vector.memset(attn_s[:], 0.0)
        nc.vector.memset(state[:, 0], 0.0).then_inc(normed_done, 1)
        dve.wait_ge(consts_in, 16 * 8)
        link(nc.vector.tensor_tensor(lb_max[:], lb_pair[:, 0, :], lb_pair[:, 1, :], ALU.max))
        nc.vector.tensor_tensor(lb_pair[:], lb_pair[:], lb_max[:].unsqueeze(1).broadcast_to([P, 2, HEADS]),
                                ALU.subtract).then_inc(lb_shifted, 1)
        dve.wait_ge(lb_exps, 1)
        link(nc.vector.tensor_tensor(lb_sum[:], lb_pair[:, 0, :], lb_pair[:, 1, :], ALU.add))
        link(nc.vector.reciprocal(lb_sum[:], lb_sum[:]))
        link(nc.vector.tensor_tensor(lb[:], lb_pair[:, 0, :], lb_sum[:], ALU.mult))
        link(nc.vector.tensor_scalar(lb_rest[:], lb[:], -1.0, 1.0, ALU.mult, ALU.add))
        order.restart()

        def gates(n, s, w, chunk, resets):
            nch = w // chunk
            by_chunk = lambda a: a[:, :, 0:w].rearrange("p h (c t) -> p (h c) t", t=chunk) if w == P else a[:, :, 0:w].rearrange("p h (c t) -> p h c t", t=chunk)
            dve.wait_ge(sig_done, n + 1)
            for h in range(HEADS):
                ins = nc.vector.tensor_scalar(forget[:, h, 0:w], forget[:, h, 0:w], lb_rest[:, h:h + 1], lb[:, h:h + 1],
                                              ALU.mult, ALU.add)
            ins.then_inc(f_done, 1)
            dve.wait_ge(f_done, n + 1)
            nc.vector.tensor_scalar(key[:, :, 0:w], forget[:, :, 0:w], -1.0, 1.0, ALU.mult, ALU.add)
            dve.wait_ge(log_done, n + 1)
            for h in range(HEADS):
                ins = nc.vector.tensor_tensor_scan(cum[:, h, 0:w], resets[:], logf[:, h, 0:w], 0.0, ALU.mult, ALU.add)
            link(ins)
            for h in range(HEADS):
                ch = lambda a: a[:, h, 0:w].rearrange("p (c t) -> p c t", t=chunk)
                mid, end = ch(cum)[:, :, chunk // 2 - 1:chunk // 2], ch(cum)[:, :, chunk - 1:chunk]
                nc.vector.tensor_tensor(ch(cum_mid), ch(cum), mid.broadcast_to([P, nch, chunk]), ALU.subtract)
                ins = nc.vector.tensor_tensor(ch(cum_end), end.broadcast_to([P, nch, chunk]), ch(cum), ALU.subtract)
            ins.then_inc(cum_done, 1)
            dve.wait_ge(exps_done, n + 1)
            for h in range(HEADS):
                ins = nc.vector.tensor_copy(decay[:, h * nch:(h + 1) * nch],
                                            e_in[:, h, 0:w].rearrange("p (c t) -> p c t", t=chunk)[:, :, chunk - 1])
            link(ins)
            link(nc.vector.tensor_tensor(e_out[:, :, 0:w], e_out[:, :, 0:w], key[:, :, 0:w], ALU.mult))
            nc.vector.tensor_tensor(e_in[:, :, 0:w], e_in[:, :, 0:w], q_in[:, s, :, 0:w], ALU.mult)
            nc.vector.tensor_tensor(e_q[:, :, 0:w], e_q[:, :, 0:w], q_in[:, s, :, 0:w], ALU.mult)
            nc.vector.tensor_tensor(e_k[:, :, 0:w], e_k[:, :, 0:w], key[:, :, 0:w], ALU.mult).then_inc(scaled_done, 1)

        def head_norm(n, s, w):
            dve.wait_ge(roots_done, n + 1)
            link(nc.vector.reciprocal(rstd[:, :, 0:w], root[:, :, 0:w]))
            dve.wait_ge(oa_out, n + START)
            link(nc.vector.scalar_tensor_tensor(out=normed[:, s, :, 0:w], in0=out[:, :, 0:w], scalar=head_w[:, 0:1],
                                                in1=rstd[:, :, 0:w], op0=ALU.mult, op1=ALU.mult))
            nc.vector.tensor_tensor(normed[:, s, :, 0:w], normed[:, s, :, 0:w], g_in[:, s, :, 0:w], ALU.mult).then_inc(normed_done, 1)

        def run(n, i, s):
            gates(n, s, P, CHUNK, reset)
            dve.wait_ge(pe_turned, n + 1)
            nc.vector.tensor_copy(k_rows[:], turned[:])
            nc.vector.copy_predicated(attn[:], causal[:], scores[:, 0:HEADS * CHUNK].rearrange("p (h t) -> p h t", h=HEADS)).then_inc(rows_copied, 1)
            for c in range(N_CH):
                dve.wait_ge(updates_done, n * N_CH + (c + 1))
                if c:
                    dve.wait_ge(state_done, n * N_CH + c + START)
                dve.wait_ge(chunk_done, n * N_CH + c + START)
                for h in range(HEADS):
                    ins = nc.vector.scalar_tensor_tensor(
                        out=state[:, (c + 1) % 2, h, :], in0=state[:, c % 2, h, :], scalar=decay[:, h * N_CH + c:h * N_CH + c + 1],
                        in1=update[:, c % 2, h * P:(h + 1) * P], op0=ALU.mult, op1=ALU.add)
                ins.then_inc(state_done, 1)
            head_norm(n, s, P)
            order.restart()

        all_tiles(dve, run)
        gates(N_P, 0, S_TOK, DEC_T, reset_s)
        dve.wait_ge(pe_turned, N_P + 1)
        nc.vector.tensor_copy(k_rows[0:S_TOK], turned[0:S_TOK])
        nc.vector.copy_predicated(attn_s[:], causal_s[:], scores[0:S_TOK, 0:HEADS * S_TOK].rearrange("p (h t) -> p h t", h=HEADS)).then_inc(rows_copied, 1)
        dve.wait_ge(s_in, 16)
        for b in range(DEC_B):
            if b >= 2:
                dve.wait_ge(update_s, b - 1)
            nc.vector.tensor_scalar(v_one[b % 2], v_in[0:S_TOK, 0, :], own_row[:, b:b + 1], None, ALU.mult).then_inc(state_done, 1)
            dve.wait_ge(update_s, b + 1)
            if b >= 2:
                dve.wait_ge(state_stored[b % 2], 16 * (b // 2))
            for h in range(HEADS):
                ins = nc.vector.scalar_tensor_tensor(
                    out=state_out[:, b % 2, h, :], in0=state_in[:, b, h, :], scalar=decay[:, h * DEC_B + b:h * DEC_B + b + 1],
                    in1=update[:, b % 2, h * P:(h + 1) * P], op0=ALU.mult, op1=ALU.add)
            ins.then_inc(s_row, 1)
        head_norm(N_P, 0, S_TOK)

    @block.tensor
    def _(pe):
        ident, ones = const["ident"], const["ones"]

        def norm_sums(n, w):
            pe.wait_ge(squares, n + 1)
            if w == P:
                nc.tensor.matmul(sums[:].rearrange("p h t -> p (h t)"), ones[:], square[:].rearrange("p h t -> p (h t)"),
                                 start=True, stop=True).then_inc(sums_done, 1)
            else:
                for h in range(HEADS):
                    ins = nc.tensor.matmul(sums[:, h, 0:w], ones[:], square[:, h, 0:w], start=True, stop=True)
                ins.then_inc(sums_done, 1)

        def keys_and_scores(n):
            pe.wait_ge(scaled_done, n + 1)
            pe.wait_ge(normed_done, n + 1 + START)
            for h in range(HEADS):
                nc.tensor.transpose(turned[:, h, :], e_out[:, h, :], ident[:])
            for h in range(HEADS):
                for c in range(N_CH):
                    t = slice(c * CHUNK, (c + 1) * CHUNK)
                    ins = nc.tensor.matmul(scores[t, h * CHUNK:(h + 1) * CHUNK], e_k[:, h, t], e_q[:, h, t], start=True, stop=True)
            ins.then_inc(pe_turned, 1)

        def state_update(n, s, c):
            t = slice(c * CHUNK, (c + 1) * CHUNK)
            for h in range(HEADS):
                ins = nc.tensor.matmul(update[:, c % 2, h * P:(h + 1) * P], k_rows[t, h, :], v_in[t, s, h * P:(h + 1) * P],
                                       start=True, stop=True)
            ins.then_inc(updates_done, 1)

        def first_updates(n, s):
            pe.wait_ge(rows_copied, n + 1)
            pe.wait_ge(state_done, n * N_CH + START)
            state_update(n, s, 0)
            state_update(n, s, 1)

        def chunk(n, s, c):
            t = slice(c * CHUNK, (c + 1) * CHUNK)
            pe.wait_ge(state_done, n * N_CH + c + START)
            pe.wait_ge(chunk_done, n * N_CH + c + START)
            for h in range(HEADS):
                nc.tensor.matmul(out[:, h, t], v_in[t, s, h * P:(h + 1) * P], attn[t, h, :], start=True, stop=False)
                ins = nc.tensor.matmul(out[:, h, t], state[:, c % 2, h, :], e_in[:, h, t], start=False, stop=True)
            ins.then_inc(chunk_done, 1)
            if c + 2 < N_CH:
                pe.wait_ge(state_done, n * N_CH + (c + 1) + START)
                state_update(n, s, c + 2)

        def sample_keys_and_scores():
            pe.wait_ge(scaled_done, N_P + 1)
            pe.wait_ge(normed_done, N_P + 1 + START)
            for h in range(HEADS):
                nc.tensor.transpose(turned[0:S_TOK, h, :], e_out[:, h, 0:S_TOK], ident[:])
            for h in range(HEADS):
                ins = nc.tensor.matmul(scores[0:S_TOK, h * S_TOK:(h + 1) * S_TOK], e_k[:, h, 0:S_TOK], e_q[:, h, 0:S_TOK],
                                       start=True, stop=True)
            ins.then_inc(pe_turned, 1)

        def sample_outputs():
            pe.wait_ge(rows_copied, N_P + 1)
            pe.wait_ge(s_in, 16)
            for h in range(HEADS):
                nc.tensor.matmul(out[:, h, 0:S_TOK], v_in[0:S_TOK, 0, h * P:(h + 1) * P], attn_s[:, h, :], start=True, stop=False)
                for b in range(DEC_B):
                    t = slice(b * DEC_T, (b + 1) * DEC_T)
                    ins = nc.tensor.matmul(out[:, h, t], state_in[:, b, h, :], e_in[:, h, t], start=False, stop=(b == DEC_B - 1))
            ins.then_inc(chunk_done, N_CH)

        def sample_update(b):
            pe.wait_ge(state_done, N_P * N_CH + b + 1 + START)
            if b >= 2:
                pe.wait_ge(s_row, b - 1)
            for h in range(HEADS):
                ins = nc.tensor.matmul(update[:, b % 2, h * P:(h + 1) * P], k_rows[0:S_TOK, h, :],
                                       v_one[b % 2][:, h * P:(h + 1) * P], start=True, stop=True)
            ins.then_inc(update_s, 1)

        def run(n, s, w_round, kind, to, before, thirds, beside):
            after = {}
            if isinstance(beside, tuple):
                tile, tile_round, slot = beside
                after = {2: lambda: keys_and_scores(tile), 3: lambda: first_updates(tile, slot), 8: lambda: norm_sums(tile, P)}
                for c in range(N_CH):
                    after[4 + c] = lambda c=c: chunk(tile, slot, c)
            elif beside == "sample":
                after = {2: sample_keys_and_scores, 4: sample_outputs, 6: lambda: norm_sums(N_P, S_TOK)}
            elif beside == "sample states":
                after = {b: (lambda b=b: sample_update(b)) for b in range(DEC_B)}
            pe.wait_ge(w_split, n + 1)
            for u, unit in enumerate(units_of(kind)):
                if not (isinstance(before, int) and before + u < SLOTS):
                    pe.wait_ge(unit_copied, before + (u - SLOTS + 1))
                for c in range(DC):
                    for j, (w_part, n_part) in enumerate(((w_lo, n_hi), (w_hi, n_lo), (w_hi, n_hi))):
                        first, last = c == 0 and j == 0, c == DC - 1 and j == 2
                        if kind == "T":
                            m, t0, k = unit
                            ins = nc.tensor.matmul(acc[:, u % SLOTS, 0:k], w_part[:, s, c, m * P:(m + 1) * P],
                                                   n_part[:, c, t0:t0 + k], start=first, stop=last)
                        else:
                            t, k = unit
                            ins = nc.tensor.matmul(acc[0:k, u % SLOTS, :], n_part[:, c, t * P:t * P + k], w_part[:, s, c, :],
                                                   start=first, stop=last)
                ins.then_inc(unit_done, 1)
                if u in after:
                    after[u]()

        all_blocks(pe, run)


def shape_constants():
    out = {}
    t = np.arange(P)
    out["chunk_reset"] = np.tile((t % CHUNK != 0).astype(np.float32), (P, 1))
    ts = np.arange(S_TOK)
    out["chunk_reset_s"] = np.tile((ts % DEC_T != 0).astype(np.float32), (P, 1))
    out["chunk_causal"] = np.tile((t[:, None] % CHUNK <= np.arange(CHUNK)[None]).astype(np.int32), (1, HEADS))
    out["sample_causal"] = np.tile(((ts[:, None] // DEC_T == ts[None] // DEC_T) & (ts[:, None] <= ts[None])).astype(np.int32), (1, HEADS))
    out["own_row"] = (ts[:, None] // DEC_T == np.arange(DEC_B)[None]).astype(np.float32)
    return out


def rotate_phase(nc, ctx, sem, const, x, consts, dram, qk_t):
    sb = lambda name, shape, dt=F32: ctx.enter_context(nc.sbuf_tensor(name, shape, dt))
    NH = 2 * len(GROUPS) * HEADS
    PART = 4
    SLOTS = 3
    raw = sb("qk_raw", [P, SLOTS, NH, DH])
    square = sb("qk_square", [P, NH, DH])
    sums, roots = sb("qk_square_sums", [P, SLOTS, NH]), sb("qk_root", [P, SLOTS, NH])
    mark = sb("rotate_mark", [1, 2])
    rot = sb("rot_rows", [P, SLOTS, 2, HALF_ROT])
    weights = sb("qk_weights", [P, 2, DH])
    turns = sb("rot_parts", [P, 4, NH, HALF_ROT])
    turned = ctx.enter_context(nc.psum_tensor("qk_turned", [P, 2, PART, P], F32))
    weights_in = sem("qk_weights_in")
    loaded, kept = [sem(f"qk_in{k}") for k in range(SLOTS)], [sem(f"qk_kept{k}", START) for k in range(SLOTS)]
    roots_ready, rows_ready = sem("qk_roots"), sem("qk_rows")
    part_turned, part_copied = sem("qk_part_turned", START), sem("qk_part_copied", START)
    own, act_own = sem("rotate_own"), sem("rotate_act_own")
    ROUNDS = N_TILES // SLOTS
    assert N_TILES == ROUNDS * SLOTS
    N_PARTS = NH // PART
    block = ctx.enter_context(nc.Block())

    def all_tiles(eng, run):
        with eng.Fori(0, ROUNDS - 1) as i:
            for s in range(SLOTS):
                run(i * SLOTS + s, i, s, P)
        for s in range(SLOTS):
            run((ROUNDS - 1) * SLOTS + s, ROUNDS - 1, s, P if s < SLOTS - 1 else S_TOK)

    @block.sync
    def _(sp):
        sp.dma_start(weights[:, 0, :], x["q_norm_w"].broadcast_to([P, DH])).then_inc(weights_in, 16)
        sp.dma_start(weights[:, 1, :], x["k_norm_w"].broadcast_to([P, DH])).then_inc(weights_in, 16)

        def run(n, i, s, w):
            wait_apart(sp, part_turned, n * N_PARTS + START, weights_in, 32)
            sp.wait_ge(kept[s], i * 16 + START)
            sp.dma_start(raw[0:w, s].rearrange("p a b -> p (a b)"), dram["h_r"][bass.ds(n * P, w), R_Q:R_V]).then_inc(loaded[s], 16)
            sp.dma_start(rot[0:w, s].rearrange("p a b -> p (a b)"), consts["rot"][bass.ds(n * P, w), :]).then_inc(loaded[s], 16)

        all_tiles(sp, run)

    @block.scalar
    def _(act):
        order = Order(act, act_own)

        def measure(n, i, s):
            act.wait_ge(loaded[s], i * 32 + 32)
            if not (isinstance(n, int) and n == 0):
                act.wait_ge(rows_ready, n)
            for h in range(NH):
                ins = nc.scalar.activation(square[:, h, :], raw[:, s, h, :], ACT.Square, accum_out=sums[:, s, h:h + 1])
            order.link(ins)
            nc.scalar.activation(roots[:, s, :], sums[:, s, :], ACT.Sqrt, bias=const["eps"][:], scale=1.0 / DH).then_inc(roots_ready, 1)
            order.restart()

        def run(n, i, s, w):
            if w == P:
                measure(n + 1, i + 1 if s == SLOTS - 1 else i, (s + 1) % SLOTS)
            act.wait_ge(rows_ready, n + 2)
            act.dma_start(dram["qk"][bass.ds(n * P, w), :], raw[0:w, s].rearrange("p a b -> p (a b)")).then_inc(kept[s], 16)
            for part in range(N_PARTS):
                act.wait_ge(part_turned, n * N_PARTS + ((SLOTS - 1) * N_PARTS + part + 1) + START)
                nc.scalar.copy(qk_t[:, part * PART:(part + 1) * PART, bass.ds(n * P, w)],
                               turned[:, part % 2, :, 0:w]).then_inc(part_copied, 1)

        measure(0, 0, 0)
        all_tiles(act, run)
        for s in range(SLOTS):
            act.wait_ge(kept[s], 16 * ROUNDS + START)

    @block.vector
    def _(dve):
        order = Order(dve, own)
        link = order.link
        nc.vector.memset(mark[:, 0:1], 0.0).then_inc(part_turned, (SLOTS - 1) * N_PARTS)
        nc.vector.memset(mark[:, 1:2], 0.0).then_inc(rows_ready, 1)
        dve.wait_ge(weights_in, 32)

        def run(n, i, s, w):
            dve.wait_ge(roots_ready, n + 1)
            link(nc.vector.reciprocal(roots[0:w, s, :], roots[0:w, s, :]))
            rows = raw[0:w, s]
            link(nc.vector.tensor_tensor(rows, rows, roots[0:w, s, :].unsqueeze(2).broadcast_to([w, NH, DH]), ALU.mult))
            for j in range(2):
                half = raw[0:w, s, j * (NH // 2):(j + 1) * (NH // 2), :]
                ins = nc.vector.tensor_tensor(half, half, weights[0:w, j, :].unsqueeze(1).broadcast_to([w, NH // 2, DH]), ALU.mult)
            link(ins)
            x1, x2 = rows[:, :, 0:HALF_ROT], rows[:, :, HALF_ROT:ROT]
            cos = rot[0:w, s, 0, :].unsqueeze(1).broadcast_to([w, NH, HALF_ROT])
            sin = rot[0:w, s, 1, :].unsqueeze(1).broadcast_to([w, NH, HALF_ROT])
            nc.vector.tensor_tensor(turns[0:w, 0], x1, cos, ALU.mult)
            nc.vector.tensor_tensor(turns[0:w, 1], x2, sin, ALU.mult)
            nc.vector.tensor_tensor(turns[0:w, 2], x1, sin, ALU.mult)
            link(nc.vector.tensor_tensor(turns[0:w, 3], x2, cos, ALU.mult))
            nc.vector.tensor_tensor(x1, turns[0:w, 0], turns[0:w, 1], ALU.subtract)
            nc.vector.tensor_tensor(x2, turns[0:w, 2], turns[0:w, 3], ALU.add).then_inc(rows_ready, 1)
            order.restart()

        all_tiles(dve, run)

    @block.tensor
    def _(pe):
        def run(n, i, s, w):
            pe.wait_ge(rows_ready, n + 2)
            for part in range(N_PARTS):
                if not (isinstance(n, int) and n == 0 and part < 2):
                    pe.wait_ge(part_copied, n * N_PARTS + max(part - 1, 0) + START)
                for h in range(PART):
                    ins = nc.tensor.transpose(turned[:, part % 2, h, 0:w], raw[0:w, s, part * PART + h, :], const["ident"][0:w, 0:w])
                ins.then_inc(part_turned, 1)

        all_tiles(pe, run)


def cached(caches, g, kv, b):
    rows = caches[g][bass.ds(b, 1), kv].rearrange("b h w d -> (b h) w d")
    if g == 0:
        return rows.rearrange("h j d -> j h d")
    return rows.rearrange("h (j r) d -> j h r d", r=GROUPS[g][1])[:, :, 0:DEC_T, :]


def attention_phase(nc, ctx, sem, const, consts, dram, qk_t, caches, s_t, new_kv_p, new_kv_s):
    sb = lambda name, shape, dt=F32: ctx.enter_context(nc.sbuf_tensor(name, shape, dt))
    psum = lambda name, shape: ctx.enter_context(nc.psum_tensor(name, shape, F32))
    SCALE = float(DH) ** -0.5
    NQ = len(GROUPS) * HEADS
    q_now = sb("q_now", [P, 2, HEADS, P])
    v_now = sb("v_now", [P, 2, 2, WIDTH])
    masked = sb("masked_scores", [P, 2, HEADS, 2, P])
    probs_t = sb("probs_t", [P, HEADS, 2, P])
    mark, s_mark = sb("att_mark", [1, 1]), sb("s_scored_mark", [1, 1])
    top = sb("row_top", [P, 2, 2, HEADS])
    result = sb("att_result", [P, 2, HEADS, DH + 2])
    mask_window = sb("mask_window", [P, 2, P])
    mask_pair = sb("mask_pair", [P, 2, P])
    past = sb("past_keys", [P, 2, HEADS, DEC_T, DH])
    q_all = sb("q_broadcast", [P, 2, DEC_T, WIDTH])
    prod = sb("qk_products", [P, 2, HEADS, DEC_T, DH])
    past_in = [sem("past0_in"), sem("past1_in")]
    prods_ready, s_scored = sem("s_prods_ready"), sem("s_scored")
    assert DEC_B == 2 * 4
    scores = psum("att_scores", [P, 2, HEADS, 2, P])
    p_turned = psum("p_turned", [P, HEADS, 2, P])
    summed = psum("att_summed", [P, HEADS, DH])
    masks_in = sem("att_masks_in")
    v_in = [sem("att_v0"), sem("att_v1")]
    q_ready, scores_done, top_ready, probs_ready = sem("q_now_ready"), sem("att_scores_done"), sem("top_ready"), sem("probs_ready")
    p_turned_done, p_copied, summed_done, result_ready = sem("p_turned_done"), sem("p_copied"), sem("att_summed_done"), sem("result_ready")
    stored = [sem("att_stored0"), sem("att_stored1")]
    kv_stored = sem("kv_stored")
    own = sem("att_own")
    block = ctx.enter_context(nc.Block())

    PASSES = [(0, 1, (False, True), 0), (0, 3, (True, True), 2), (1, 4, (False, True), 0), (2, 4, (False, False), 0)]

    m_pairs = lambda befores: 0 if befores == PASSES[0][2] else PASSES[0][1]
    PAIRS_BEFORE_2 = sum(q[1] for q in PASSES if q[0] < 2)

    def all_tiles(eng, pair):
        done = 0
        for g, pairs, befores, first in PASSES:
            if pairs == 1:
                pair(done, done // 2, g, first, 0, befores)
            else:
                with eng.Fori(0, pairs) as i:
                    pair(i * 2 + done, i + done // 2, g, i * 2 + first, i, befores)
            done += 2 * pairs
        return done

    def rows_of(table, g, m, i, s, before):
        if g == 0:
            return [(slice(0, P), table[bass.ds((m - 1) * P if before else m * P, P), :])]
        if g == 1:
            half = table.rearrange("(j i r) c -> j r i c", r=GROUPS[1][1], i=P)[s - 1 if before else s]
            return [(slice(0, P), half[bass.ds(i, 1)].rearrange("r i c -> (r i) c"))]
        by = table.rearrange("(i r) c -> r i c", r=GROUPS[2][1])
        return [(slice(64 * e, 64 * e + 64), by[bass.ds(m * 2 + e, 1)].rearrange("r i c -> (r i) c")) for e in range(2)]

    def columns_of(head, g, m, i, s, before):
        if g == 0:
            return qk_t[:, head, bass.ds((m - 1) * P if before else m * P, P)].unsqueeze(1)
        if g == 1:
            r, n = GROUPS[1][1], P
            start = (s - 1 if before else s) * r * n
            return qk_t[:, head, start:start + r * n].rearrange("d (i r) -> d r i", r=r)[:, bass.ds(i, 1), :]
        r = GROUPS[2][1]
        return qk_t[:, head, 0:SEQ].rearrange("d (i r) -> d r i", r=r)[:, bass.ds(m * 2, 2), :]

    @block.sync
    def _(sp):
        sp.dma_start(mask_window[:].rearrange("p a b -> p (a b)"), consts["mask_window"]).then_inc(masks_in, 16)
        sp.dma_start(mask_pair[:].rearrange("p a b -> p (a b)"), consts["mask_pair"]).then_inc(masks_in, 16)
        n_kv = 0
        for g, (win, _) in enumerate(GROUPS):
            keep = min(win, SEQ)
            for j in range(2):
                source = (dram["qk"], (len(GROUPS) + g) * WIDTH) if j == 0 else (dram["h_r"], R_V + g * WIDTH)
                cols = source[0][:, source[1]:source[1] + WIDTH]
                sp.dma_start(new_kv_p[g][0, 0, j].rearrange("h t d -> t h d"),
                             cols[SEQ - keep:SEQ].rearrange("t (h d) -> t h d", h=HEADS)).then_inc(kv_stored, 16)
                n_kv += 1
                for h in range(HEADS):
                    sp.dma_start(new_kv_s[g][0, :, j, h],
                                 cols[SEQ:TOK, h * DH:(h + 1) * DH].rearrange("(b t) d -> b t d", b=DEC_B)).then_inc(kv_stored, 16)
                    n_kv += 1

        def pair(n, p, g, m, i, befores):
            b = i if g else i + m_pairs(befores)
            for s in range(2):
                wait_apart(sp, s_scored, n + s, masks_in, 32)
                sp.dma_start(past[:, s, :, 0, :] if g == 0 else past[:, s], cached(caches, g, 0, b * 2 + s)).then_inc(past_in[s], 16)
                sp.dma_start(q_all[:, s], dram["qk"][bass.ds(SEQ + (b * 2 + s) * DEC_T, DEC_T), g * WIDTH:(g + 1) * WIDTH]
                             .unsqueeze(0).broadcast_to([P, DEC_T, WIDTH])).then_inc(past_in[s], 16)
            for s in range(2):
                sp.wait_ge(summed_done, n + s)
                for e in range(1 + befores[s]):
                    for at, src in rows_of(dram["h_r"][0:SEQ, R_V + g * WIDTH:R_V + (g + 1) * WIDTH], g, m + s, i, s, e == 1):
                        sp.dma_start(v_now[at, s, e, :], src).then_inc(v_in[s], 16)

        all_tiles(sp, pair)
        sp.wait_ge(kv_stored, 16 * n_kv)

    def v_loads(g, befores, s):
        return 2 if g == 2 else 1 + befores[s]

    def v_loads_until(p_pass, s):
        return sum(q[1] * v_loads(q[0], q[2], s) for q in PASSES[:p_pass])

    def pass_of(g, befores):
        return next(k for k, q in enumerate(PASSES) if q[0] == g and q[2] == befores)

    @block.gpsimd
    def _(pool):
        def pair(n, p, g, m, i, befores):
            for s in range(2):
                pool.wait_ge(summed_done, n + s)
                for h in range(HEADS):
                    src = columns_of(g * HEADS + h, g, m + s, i, s, False)
                    ins = nc.gpsimd.tensor_copy(q_now[:, s, h, :].rearrange("p (a b) -> p a b", a=src.shape[1]), src)
                ins.then_inc(q_ready, 1)
            for s in range(2):
                pool.wait_ge(past_in[s], p * 32 + 32)
                pool.wait_ge(s_scored, n + s)
                keys = past[:, s, :, 0:1, :].broadcast_to([P, HEADS, DEC_T, DH]) if g == 0 else past[:, s]
                nc.gpsimd.tensor_tensor(prod[:, s], keys, q_all[:, s].rearrange("p t (h d) -> p h t d", h=HEADS),
                                        ALU.mult).then_inc(prods_ready, 1)

        all_tiles(pool, pair)

    @block.tensor
    def _(pe):
        def pair(n, p, g, m, i, befores):
            for s in range(2):
                pe.wait_ge(q_ready, n + s + 1)
                for h in range(HEADS):
                    for e in range(1 + befores[s]):
                        keys = columns_of(NQ + g * HEADS + h, g, m + s, i, s, e == 1)
                        ins = nc.tensor.matmul(scores[:, s, h, e, :].rearrange("p (a b) -> p a b", a=keys.shape[1]),
                                               q_now[:, s, h, :], keys, start=True, stop=True)
                ins.then_inc(scores_done, 1)
            for s in range(2):
                pe.wait_ge(probs_ready, n + s + 1)
                for h in range(HEADS):
                    for e in range(1 + befores[s]):
                        ins = nc.tensor.transpose(p_turned[:, h, e, :], masked[:, s, h, e, :], const["ident"][:])
                ins.then_inc(p_turned_done, 1)
                pe.wait_ge(p_copied, n + s + 1)
                k = pass_of(g, befores)
                loads = v_loads(g, befores, s)
                pe.wait_ge(v_in[s], i * (16 * loads) + 16 * (v_loads_until(k, s) + loads))
                pe.wait_ge(result_ready, n + s)
                for h in range(HEADS):
                    for e in range(1 + befores[s]):
                        ins = nc.tensor.matmul(summed[:, h, :], probs_t[:, h, e, :], v_now[:, s, e, h * DH:(h + 1) * DH],
                                               start=(e == 0), stop=(e == befores[s]))
                ins.then_inc(summed_done, 1)

        all_tiles(pe, pair)

    @block.vector
    def _(dve):
        order = Order(dve, own)
        link = order.link
        nc.vector.memset(mark[:], 0.0).then_inc(summed_done, 1)
        nc.vector.memset(s_mark[:], 0.0).then_inc(s_scored, 1)
        dve.wait_ge(masks_in, 32)

        def pair(n, p, g, m, i, befores):
            for s in range(2):
                k = 1 + befores[s]
                mask = (mask_pair if g == 2 else mask_window)[:, 0:k, :].unsqueeze(1).broadcast_to([P, HEADS, k, P])
                dve.wait_ge(scores_done, n + s + 1)
                if k == 1:
                    link(nc.vector.tensor_tensor(masked[:, s, :, 0, :], scores[:, s, :, 0, :], mask[:, :, 0, :], ALU.add))
                    link(nc.vector.tensor_reduce(top[:, s, 0, :], masked[:, s, :, 0, :], AX_X, ALU.max))
                else:
                    link(nc.vector.tensor_tensor(masked[:, s], scores[:, s], mask, ALU.add))
                    link(nc.vector.tensor_reduce(top[:, s, 0, :], masked[:, s].rearrange("p h e k -> p h (e k)"), AX_X, ALU.max))
                dve.wait_ge(stored[s], i * 32 + 16 * PAIRS_BEFORE_2 if g == 2 else p * 16)
                nc.vector.tensor_scalar(result[:, s, :, DH:DH + 1], top[:, s, 0, :].unsqueeze(2), SCALE, None, ALU.mult)
                nc.vector.tensor_scalar(top[:, s, 1, :], top[:, s, 0, :], -SCALE, None, ALU.mult).then_inc(top_ready, 1)
            b = i if g else i + m_pairs(befores)
            for s in range(2):
                dve.wait_ge(prods_ready, n + s + 1)
                nc.vector.tensor_reduce(s_t[:, g, :, bass.ds(b * 2 + s, 1), :].rearrange("p h b t -> p h (b t)"), prod[:, s],
                                        AX_X, ALU.add).then_inc(s_scored, 1)
            for s in range(2):
                dve.wait_ge(summed_done, n + s + 2)
                nc.vector.tensor_copy(result[:, s, :, 0:DH], summed[:]).then_inc(result_ready, 1)
            order.restart()

        all_tiles(dve, pair)

    @block.scalar
    def _(act):
        def pair(n, p, g, m, i, befores):
            for s in range(2):
                k = 1 + befores[s]
                act.wait_ge(top_ready, n + s + 1)
                for h in range(HEADS):
                    ins = nc.scalar.activation(masked[:, s, h, 0:k, :], masked[:, s, h, 0:k, :], ACT.Exp, bias=top[:, s, 1, h:h + 1],
                                               scale=SCALE, accum_out=result[:, s, h, DH + 1:DH + 2])
                ins.then_inc(probs_ready, 1)
            for s in range(2):
                k = 1 + befores[s]
                act.wait_ge(p_turned_done, n + s + 1)
                act.wait_ge(summed_done, n + s + 1)
                nc.scalar.copy(probs_t[:, :, 0:k, :], p_turned[:, :, 0:k, :]).then_inc(p_copied, 1)
                act.wait_ge(result_ready, n + s + 1)
                for at, dst in rows_of(dram["att"][g], g, m + s, i, s, False):
                    act.dma_start(dst, result[at, s].rearrange("p h d -> p (h d)")).then_inc(stored[s], 16)

        all_tiles(act, pair)
        for s in range(2):
            act.wait_ge(stored[s], 16 * PAIRS_BEFORE_2 + 32 * PASSES[-1][1])


def attention_constants():
    out = {}
    t = np.arange(P)
    own = np.where(t[None] <= t[:, None], 0.0, MASKED)
    before = np.where(t[None] >= t[:, None], 0.0, MASKED)
    out["mask_window"] = np.concatenate([own, before], 1).astype(np.float32)
    same = (t[None] // 64 == t[:, None] // 64) & (t[None] <= t[:, None])
    out["mask_pair"] = np.concatenate([np.where(same, 0.0, MASKED), before], 1).astype(np.float32)
    inv = (THETA ** (-np.arange(0, ROT, 2, dtype=np.float32) / np.float32(ROT))).astype(np.float32)
    pos = np.concatenate([np.arange(SEQ), np.tile(PAST + np.arange(DEC_T), DEC_B)]).astype(np.float32)
    ang = (pos[:, None] * inv[None]).astype(np.float32)
    out["rot"] = np.concatenate([np.cos(ang), np.sin(ang)], 1).astype(np.float32)
    return out


def merge_phase(nc, ctx, sem, const, caches, consts, dram, qk_t, s_t):
    sb = lambda name, shape, dt=F32: ctx.enter_context(nc.sbuf_tensor(name, shape, dt))
    psum = lambda name, shape: ctx.enter_context(nc.psum_tensor(name, shape, F32))
    SCALE = float(DH) ** -0.5
    G = len(GROUPS)
    N_BACK = P
    V_SLOTS = 8
    past = sb("past_rows", [P, V_SLOTS, HEADS, DEC_T, DH])
    v_new = sb("v_new", [S_TOK, G, WIDTH])
    mask = sb("mask_sample", [P, G, N_BACK + S_TOK])
    probs = sb("probs_s", [P, G, N_BACK + S_TOK])
    stat = sb("stat_s", [P, 4])
    probs_t = sb("probs_past_t", [P, G, P])
    new_t = sb("probs_new_t", [S_TOK, G, P])
    o_t = sb("o_sample_t", [P, HEADS, S_TOK])
    scores = psum("scores_s", [P, G, N_BACK + S_TOK])
    p_turned = psum("p_past_turned", [P, G, P])
    n_turned = psum("p_new_turned", [S_TOK, G, P])
    summed = psum("summed_s", [P, P])
    consts_in = sem("s_att_consts_in")
    values_in = [sem(f"past_values{k}_in") for k in range(V_SLOTS)]
    rows_scored, masked_ready, shift_ready = sem("s_rows_scored"), sem("s_masked"), sem("s_shift_ready")
    exps_ready, probs_ready, s_turned_done, copied, added = sem("s_exps_ready"), sem("s_probs_ready"), sem("s_p_turned"), sem("s_p_copied"), sem("s_values_added")
    summed_done, o_ready, o_stored = sem("s_summed_done"), sem("s_o_ready"), sem("s_o_stored")
    s_own = sem("s_att_own")
    parts = sb("att_parts", [P, 2, G, HEADS, DH + 2])
    top = sb("merge_top", [P, 2, HEADS])
    scale = sb("merge_scale", [P, 2, G, HEADS])
    dens = sb("merge_dens", [P, G, HEADS])
    den = sb("merge_den", [P, HEADS])
    mark = sb("merge_mark", [1, 1])
    merged = sb("merged", [P, 2, HEADS, DH])
    out = sb("ob_stage", [P, 2, HEADS, P])
    turned = ctx.enter_context(nc.psum_tensor("ob_turned", [P, 2, HEADS, P], F32))
    in_, stored = [sem("parts0_in"), sem("parts1_in")], [sem("ob0_stored", START), sem("ob1_stored", START)]
    shifted, exps, merged_ready, turned_done, out_ready = sem("merge_shifted"), sem("merge_exps"), sem("merged_ready", START), sem("ob_turned_done"), sem("ob_ready")
    own = sem("merge_own")
    N = SEQ // P
    block = ctx.enter_context(nc.Block())

    def all_tiles(eng, run):
        with eng.Fori(0, N // 2) as i:
            for s in range(2):
                run(i * 2 + s, i, s)

    def past_dst(g, s):
        return past[:, s, :, 0, :] if g == 0 else past[:, s]

    def load_values(eng, g, first):
        for b in range(first, DEC_B, 2):
            if g:
                eng.wait_ge(added, (g - 1) * DEC_B + b + 2)
            eng.dma_start(past_dst(g, b), cached(caches, g, 1, b)).then_inc(values_in[b], 16)

    @block.sync
    def _(sp):
        sp.dma_start(mask[:].rearrange("p a b -> p (a b)"), consts["mask_sample"]).then_inc(consts_in, 16)
        sp.dma_start(v_new[:].rearrange("p a b -> p (a b)"), dram["h_r"][SEQ:TOK, R_V:R_V + G * WIDTH]).then_inc(consts_in, 16)

        def run(n, i, s):
            sp.wait_ge(merged_ready, n + START)
            for g in range(G):
                sp.dma_start(parts[:, s, g].rearrange("p h d -> p (h d)"), dram["att"][g][bass.ds(n * P, P), :]).then_inc(in_[s], 16)

        load_values(sp, 0, 1)
        load_values(sp, 1, 1)
        all_tiles(sp, run)
        load_values(sp, 2, 1)

    @block.gpsimd
    def _(pool):
        for g in range(G):
            load_values(pool, g, 0)

    @block.vector
    def _(dve):
        order = Order(dve, s_own)
        link = order.link
        dve.wait_ge(consts_in, 32)
        dve.wait_ge(rows_scored, 1)
        link(nc.vector.tensor_tensor(probs[:], scores[:], mask[:], ALU.add))
        link(nc.vector.tensor_reduce(stat[:, 0:1], probs[:].rearrange("p a b -> p (a b)"), AX_X, ALU.max))
        nc.vector.tensor_scalar(stat[:, 1:2], stat[:, 0:1], -SCALE, None, ALU.mult).then_inc(shift_ready, 1)
        dve.wait_ge(exps_ready, 1)
        link(nc.vector.reciprocal(stat[:, 2:3], stat[:, 2:3]))
        nc.vector.tensor_scalar(probs[:], probs[:], stat[:, 2:3], None, ALU.mult).then_inc(probs_ready, 1)
        dve.wait_ge(s_turned_done, 1)
        nc.vector.tensor_copy(probs_t[:], p_turned[:])
        nc.vector.tensor_copy(new_t[:], n_turned[:]).then_inc(copied, 1)
        order = Order(dve, own)
        link = order.link
        nc.vector.memset(mark[:], 0.0).then_inc(merged_ready, 1)

        def run(n, i, s):
            tops = parts[:, s, :, :, DH]
            dve.wait_ge(in_[s], i * (16 * G) + 16 * G)
            link(nc.vector.tensor_tensor(top[:, s, :], tops[:, 0, :], tops[:, 1, :], ALU.max))
            link(nc.vector.tensor_tensor(top[:, s, :], top[:, s, :], tops[:, 2, :], ALU.max))
            nc.vector.tensor_tensor(scale[:, s], tops, top[:, s, :].unsqueeze(1).broadcast_to([P, G, HEADS]), ALU.subtract).then_inc(shifted, 1)
            dve.wait_ge(exps, n + 1)
            link(nc.vector.tensor_tensor(dens[:], scale[:, s], parts[:, s, :, :, DH + 1], ALU.mult))
            link(nc.vector.tensor_reduce(den[:], dens[:].rearrange("p g h -> p h g"), AX_X, ALU.add))
            link(nc.vector.reciprocal(den[:], den[:]))
            link(nc.vector.tensor_tensor(scale[:, s], scale[:, s], den[:].unsqueeze(1).broadcast_to([P, G, HEADS]), ALU.mult))
            for g in range(G):
                part = parts[:, s, g, :, 0:DH]
                ins = nc.vector.tensor_tensor(part, part, scale[:, s, g, :].unsqueeze(2).broadcast_to([P, HEADS, DH]), ALU.mult)
            link(ins)
            link(nc.vector.tensor_tensor(merged[:, s], parts[:, s, 0, :, 0:DH], parts[:, s, 1, :, 0:DH], ALU.add))
            nc.vector.tensor_tensor(merged[:, s], merged[:, s], parts[:, s, 2, :, 0:DH], ALU.add).then_inc(merged_ready, 1)
            dve.wait_ge(turned_done, n + 1)
            dve.wait_ge(stored[s], i * 16 + START)
            nc.vector.tensor_copy(out[:, s], turned[:, s]).then_inc(out_ready, 1)
            order.restart()
        all_tiles(dve, run)
        dve.wait_ge(summed_done, 1)
        nc.vector.tensor_copy(o_t[:].rearrange("p h t -> p (h t)"), summed[:]).then_inc(o_ready, 1)

    @block.scalar
    def _(act):
        act.wait_ge(shift_ready, 1)
        nc.scalar.activation(probs[:], probs[:], ACT.Exp, bias=stat[:, 1:2], scale=SCALE, accum_out=stat[:, 2:3]).then_inc(exps_ready, 1)
        def run(n, i, s):
            act.wait_ge(shifted, n + 1)
            nc.scalar.activation(scale[:, s], scale[:, s], ACT.Exp).then_inc(exps, 1)
            act.wait_ge(out_ready, n + 1)
            act.dma_start(dram["ob_t"][:, bass.ds(n * P, P)].rearrange("(h p) t -> p h t", p=P), out[:, s]).then_inc(stored[s], 16)
        all_tiles(act, run)
        for s in range(2):
            act.wait_ge(stored[s], 16 * (N // 2) + START)
        act.wait_ge(o_ready, 1)
        act.dma_start(dram["ob_t"][:, SEQ:TOK].rearrange("(h p) t -> p h t", p=P), o_t[:]).then_inc(o_stored, 16)
        act.wait_ge(o_stored, 16)

    @block.tensor
    def _(pe):
        NQ = G * HEADS
        for g in range(G):
            nc.tensor.transpose(scores[:, g, 0:N_BACK], s_t[:, g].rearrange("p h b t -> p (h b t)"), const["ident"][:])
        for g in range(G):
            for h in range(HEADS):
                ins = nc.tensor.matmul(scores[h * S_TOK:(h + 1) * S_TOK, g, N_BACK:], qk_t[:, g * HEADS + h, SEQ:TOK],
                                       qk_t[:, NQ + g * HEADS + h, SEQ:TOK], start=True, stop=True)
        ins.then_inc(rows_scored, 1)
        pe.wait_ge(probs_ready, 1)
        for g in range(G):
            nc.tensor.transpose(p_turned[:, g, :], probs[:, g, 0:N_BACK], const["ident"][:])
        for g in range(G):
            ins = nc.tensor.transpose(n_turned[:, g, :], probs[:, g, N_BACK:], const["ident"][:])
        ins.then_inc(s_turned_done, 1)
        nc.tensor.matmul(summed[:], const["zeros"][:, 0:P], const["zeros"][:, 0:P], start=True, stop=False).then_inc(added, 1)
        pe.wait_ge(copied, 1)
        pe.wait_ge(consts_in, 32)
        for g in range(G):
            for h in range(HEADS):
                r = slice(h * S_TOK, (h + 1) * S_TOK)
                nc.tensor.matmul(summed[:, r], v_new[:, g, h * DH:(h + 1) * DH], new_t[:, g, r], start=False, stop=False)
        def add_values(g):
            for b in range(DEC_B):
                pe.wait_ge(values_in[b], 16 * (g + 1))
                for h in range(HEADS):
                    at = b * DEC_T + h * S_TOK
                    if g == 0:
                        ins = nc.tensor.matmul(summed[:, at:at + DEC_T], past[:, b, h, 0, :], probs_t[:, g, at:at + DEC_T],
                                               start=False, stop=False)
                        continue
                    for t in range(DEC_T):
                        ins = nc.tensor.matmul(summed[:, at + t:at + t + 1], past[:, b, h, t, :], probs_t[:, g, at + t:at + t + 1],
                                               start=False, stop=False)
                ins.then_inc(added, 1)

        add_values(0)
        add_values(1)

        def run(n, i, s):
            pe.wait_ge(merged_ready, n + 2 + START)
            for h in range(HEADS):
                ins = nc.tensor.transpose(turned[:, s, h, :], merged[:, s, h, :], const["ident"][:])
            ins.then_inc(turned_done, 1)

        all_tiles(pe, run)
        add_values(2)
        nc.tensor.matmul(summed[:], const["zeros"][:, 0:P], const["zeros"][:, 0:P], start=False, stop=True).then_inc(summed_done, 1)


def mix_phase(nc, ctx, sem, const, x, dram, src_rows):
    sb = lambda name, shape, dt=F32: ctx.enter_context(nc.sbuf_tensor(name, shape, dt))
    psum = lambda name, shape: ctx.enter_context(nc.psum_tensor(name, shape, F32))
    NB = SEQ // BLOCK
    w_a, w_b, w_o = sb("w_branch_a", [P, HEADS, D]), sb("w_branch_b", [P, HEADS, D]), sb("w_out", [P, DC, D])
    gates = sb("branch_gates", [P, 2, DC, BLOCK])
    o_a, o_b = sb("o_a", [P, HEADS, BLOCK]), sb("o_b", [P, HEADS, BLOCK])
    part_a, part_b = sb("part_a", [P, 2, BLOCK]), sb("part_b", [P, 2, BLOCK])
    mix = sb("mix_t", [P, DC, BLOCK])
    mark = sb("mix_mark", [1, 2])
    rows, rows_out = sb("x_rows", [P, 2, D]), sb("x1_rows_out", [P, 2, D])
    gate_p, gate_s = sb("gate1_p", [P, D]), sb("gate1_s", [S_TOK, D])
    y = psum("branch_acc", [P, 2, 2, BLOCK])
    out = psum("mix_acc", [P, 2, D])
    w_in_, w_out_in, gate1_in, in_ = sem("branch_w_in"), sem("w_out_in"), sem("gate1_in"), sem("branch_o_in")
    gates_in, gates_done = sem("branch_gates_in"), sem("branch_gates_done")
    y_done, mixed, out_done, x1_ready = sem("branch_done"), sem("mixed"), sem("mix_out_done"), sem("x1_ready", START)
    rows_in, stored = [sem("x0_in"), sem("x1_in")], [sem("x1_stored0", START), sem("x1_stored1", START)]
    own = sem("mix_own")
    block = ctx.enter_context(nc.Block())
    view = lambda name, cols: dram[name][:, cols].rearrange("(h p) t -> p h t", p=P)

    def all_blocks(eng, run):
        with eng.Fori(0, NB) as i:
            run(i, bass.ds(i * BLOCK, BLOCK), BLOCK, i * (BLOCK // P), BLOCK // P)
        run(NB, slice(SEQ, TOK), S_TOK, SEQ // P, 1)

    def tiles(before, count, n):
        for t in range(count):
            yield t, before + t, t % 2, min(n, P)

    @block.sync
    def _(sp):
        for dst, src in ((w_a, "w_branch_a"), (w_b, "w_branch_b")):
            sp.dma_start(dst[:], x[src][0].rearrange("(c p) n -> p c n", p=P)).then_inc(w_in_, 16)

        def run(i, cols, n, before, count):
            sp.wait_ge(mixed, i * DC + 1)
            sp.dma_start(o_a[:, :, 0:n], view("oa_t", cols)).then_inc(in_, 16)
            sp.dma_start(o_b[:, :, 0:n], view("ob_t", cols)).then_inc(in_, 16)
            gates_dram = dram["h_t"][T_GATE:T_GATE + 2 * D, cols].rearrange("(j p) t -> p j t", p=P)
            sp.dma_start(gates[:, :, :, 0:n].rearrange("p a c t -> p (a c) t"), gates_dram).then_inc(gates_in, 16)
            for t, at, s, w in tiles(before, count, n):
                sp.wait_ge(x1_ready, at + START)
                sp.dma_start(rows[0:w, s, :], src_rows(at, w)).then_inc(rows_in[s], 16)

        all_blocks(sp, run)

    @block.scalar
    def _(act):
        act.dma_start(w_o[:], x["w_out"][0].rearrange("(c p) n -> p c n", p=P)).then_inc(w_out_in, 16)
        act.dma_start(gate_p[:], dram["mod"][0:1, 2 * D:3 * D].broadcast_to([P, D])).then_inc(gate1_in, 16)
        for b in range(DEC_B):
            act.dma_start(gate_s[b * DEC_T:(b + 1) * DEC_T, :], dram["mod"][b + 1:b + 2, 2 * D:3 * D].broadcast_to([DEC_T, D])).then_inc(gate1_in, 16)

        def run(i, cols, n, before, count):
            act.wait_ge(gates_in, i * 16 + 16)
            for m in range(DC):
                nc.scalar.activation(gates[:, :, m, 0:n], gates[:, :, m, 0:n], ACT.Sigmoid).then_inc(gates_done, 1)
            for t, at, s, w in tiles(before, count, n):
                act.wait_ge(x1_ready, at + 2 + START)
                act.dma_start(dram["x1"][bass.ds(at * P, w), :], rows_out[0:w, s, :]).then_inc(stored[s], 16)
        all_blocks(act, run)
        act.wait_ge(stored[0], 16 * (SEQ // P // 2 + 1) + START)
        act.wait_ge(stored[1], 16 * (SEQ // P // 2) + START)

    @block.vector
    def _(dve):
        order = Order(dve, own)
        link = order.link
        nc.vector.memset(mark[:, 0:1], 0.0).then_inc(x1_ready, 1)
        nc.vector.memset(mark[:, 1:2], 0.0).then_inc(mixed, 1)
        dve.wait_ge(gate1_in, 16 * (1 + DEC_B))

        def run(i, cols, n, before, count):
            for m in range(DC):
                s = m % 2
                dve.wait_ge(gates_done, i * DC + (m + 1))
                dve.wait_ge(y_done, i * DC + (m + 1))
                nc.vector.tensor_tensor(part_a[:, s, 0:n], gates[:, 0, m, 0:n], y[:, s, 0, 0:n], ALU.mult)
                link(nc.vector.tensor_tensor(part_b[:, s, 0:n], gates[:, 1, m, 0:n], y[:, s, 1, 0:n], ALU.mult))
                nc.vector.tensor_tensor(mix[:, m, 0:n], part_a[:, s, 0:n], part_b[:, s, 0:n], ALU.add).then_inc(mixed, 1)
            for t, at, s, w in tiles(before, count, n):
                gate = gate_p if n == BLOCK else gate_s
                dve.wait_ge(out_done, at + 1)
                dve.wait_ge(rows_in[s], i * (16 * (BLOCK // P // 2)) + 16 * (t // 2 + 1))
                dve.wait_ge(stored[s], i * (16 * (BLOCK // P // 2)) + 16 * (t // 2) + START)
                link(nc.vector.tensor_tensor(rows_out[0:w, s, :], gate[0:w, :], out[0:w, s, :], ALU.mult))
                nc.vector.tensor_tensor(rows_out[0:w, s, :], rows_out[0:w, s, :], rows[0:w, s, :], ALU.add).then_inc(x1_ready, 1)
            order.restart()
        all_blocks(dve, run)

    @block.tensor
    def _(pe):
        pe.wait_ge(w_in_, 32)

        def run(i, cols, n, before, count):
            pe.wait_ge(in_, i * 32 + 32)
            for m in range(DC):
                if m >= 2:
                    pe.wait_ge(mixed, i * DC + m)
                for j, (w, o) in enumerate(((w_a, o_a), (w_b, o_b))):
                    for c in range(HEADS):
                        ins = nc.tensor.matmul(y[:, m % 2, j, 0:n], w[:, c, m * P:(m + 1) * P], o[:, c, 0:n],
                                               start=(c == 0), stop=(c == HEADS - 1))
                ins.then_inc(y_done, 1)
            pe.wait_ge(mixed, i * DC + (DC + 1))
            pe.wait_ge(w_out_in, 16)
            for t, at, s, w in tiles(before, count, n):
                pe.wait_ge(x1_ready, at + START)
                for half in range(D // BLOCK):
                    for c in range(DC):
                        ins = nc.tensor.matmul(out[0:w, s, half * BLOCK:(half + 1) * BLOCK], mix[:, c, t * P:t * P + w],
                                               w_o[:, c, half * BLOCK:(half + 1) * BLOCK], start=(c == 0), stop=(c == DC - 1))
                ins.then_inc(out_done, 1)
        all_blocks(pe, run)


def query_phase(nc, ctx, sem, const, x, dram, n_hi, n_lo):
    sb = lambda name, shape, dt=F32: ctx.enter_context(nc.sbuf_tensor(name, shape, dt))
    psum = lambda name, shape: ctx.enter_context(nc.psum_tensor(name, shape, F32))
    QD = 2 * P
    w = sb("wq_block", [P, 2, DC, QD])
    w_hi, w_lo = sb("wq_hi", [P, 2, DC, QD], F32R), sb("wq_lo", [P, 2, DC, QD], F32R)
    w_split, split_own = sem("wq_split"), sem("wq_split_own")
    keys = sb("peer_keys", [P, 2, PH, P])
    keys_t = sb("peer_keys_t", [P, PH, 2, P])
    key_w = sb("peer_key_w", [P, 2])
    q_t = sb("peer_q_t", [P, 2, 2, TOK])
    square = sb("peer_q_square", [P, 2, 2, TOK])
    stat = sb("peer_q_stat", [P, 2, N_TILES])
    mark = sb("query_mark", [1, 1])
    stage = sb("score_stage", [P, N_TILES, QD])
    acc = psum("peer_q_acc", [P, 3, BLOCK])
    sums = psum("peer_q_sums", [P, N_TILES])
    scores = psum("peer_scores", [P, 3, BLOCK])
    turned = psum("peer_keys_turned", [P, 2, P])
    keys_in, key_turned, key_copied = sem("peer_keys_in"), sem("peer_key_turned"), sem("peer_key_copied")
    w_in_ = [sem("wq0_in"), sem("wq1_in")]
    q_done, q_copied, sums_done, roots_done, rstd_done = sem("peer_q_done", START), sem("peer_q_copied"), sem("peer_q_sums_done", START), sem("peer_q_roots_done", START), sem("peer_q_rstd", START)
    squared = sem("peer_q_squared", START)
    scored, score_copied = sem("peer_scored", START), sem("peer_score_copied", START)
    stored = [sem(f"scores_stored{k}", START) for k in range(N_TILES)]
    own = sem("query_own")
    block = ctx.enter_context(nc.Block())
    PIECES = ((0, 512), (512, 512), (SEQ, S_TOK))
    width = lambda t: P if t < N_TILES - 1 else S_TOK
    w_dram = x["peer_wq"][0].rearrange("(c p) n -> p c n", p=P)

    def heads(eng, query, norm, rest):
        query(0, 0, 0, 0)
        query(0, 0, 0, 1)
        with eng.Fori(0, PH // 2 - 1) as i:
            for s in range(2):
                query(i * 2 + (s + 1), i + s, 1 - s, 0)
                norm(i * 2 + s, s)
                query(i * 2 + (s + 1), i + s, 1 - s, 1)
                rest(i * 2 + s, s)
        query(PH - 1, PH // 2 - 1, 1, 0)
        norm(PH - 2, 0)
        query(PH - 1, PH // 2 - 1, 1, 1)
        rest(PH - 2, 0)
        norm(PH - 1, 1)
        rest(PH - 1, 1)

    @block.sync
    def _(sp):
        sp.dma_start(keys[:, 0], x["peer_k1"][0].rearrange("h n d -> n h d")).then_inc(keys_in, 16)
        sp.dma_start(keys[:, 1], x["peer_k2"][0].rearrange("h n d -> n h d")).then_inc(keys_in, 16)
        with nc.allow_non_contiguous_dma("a weight for each column"):
            sp.dma_start(key_w[:], x["peer_qn_w"].rearrange("a (j p) -> p (a j)", p=P)).then_inc(keys_in, 16)

        def query(h, i, s, j):
            if j:
                return
            if not (isinstance(h, int) and h < 2):
                sp.wait_ge(q_done, h * 6 - 6 + START)
            sp.dma_start(w[:, s], w_dram[:, :, bass.ds(h * QD, QD)]).then_inc(w_in_[s], 16)

        heads(sp, query, lambda h, s: None, lambda h, s: None)

    @block.gpsimd
    def _(pool):
        def query(h, i, s, j):
            if j:
                return
            wait_apart(pool, w_in_[s], i * 16 + 16, const["ready"], 3)
            nc.gpsimd.tensor_copy(w_hi[:, s], w[:, s]).then_inc(split_own, 1)
            pool.wait_ge(split_own, 1)
            nc.gpsimd.tensor_tensor(w_lo[:, s], w[:, s], w_hi[:, s].bitcast(F32), ALU.subtract).then_inc(w_split, 1)
            pool.sem_clear(split_own)

        heads(pool, query, lambda h, s: None, lambda h, s: None)

    @block.tensor
    def _(pe):
        pe.wait_ge(keys_in, 48)
        for h in range(PH):
            if h:
                pe.wait_ge(key_copied, h)
            for j in range(2):
                ins = nc.tensor.transpose(turned[:, j, :], keys[:, j, h, :], const["ident"][:])
            ins.then_inc(key_turned, 1)
        pe.wait_ge(key_copied, PH)

        def query(h, i, s, j):
            pe.wait_ge(w_split, h + 1)
            if not (isinstance(h, int) and h == 0 and j == 0):
                pe.wait_ge(q_copied, h * 6 + 3 * j)
            for k, (t0, n) in enumerate(PIECES):
                for c in range(DC):
                    for e, (w_part, n_part) in enumerate(((w_lo, n_hi), (w_hi, n_lo), (w_hi, n_hi))):
                        ins = nc.tensor.matmul(acc[:, k, 0:n], w_part[:, s, c, j * P:(j + 1) * P], n_part[:, c, t0:t0 + n],
                                               start=(c == 0 and e == 0), stop=(c == DC - 1 and e == 2))
                ins.then_inc(q_done, 1)

        def norm(h, s):
            pe.wait_ge(squared, h * 6 + 6 + START)
            if not (isinstance(h, int) and h == 0):
                pe.wait_ge(roots_done, h + START)
            for t in range(N_TILES):
                for j in range(2):
                    ins = nc.tensor.matmul(sums[0:width(t), t:t + 1], square[:, s, j, t * P:t * P + width(t)], const["ones"][:, 0:1],
                                           start=(j == 0), stop=(j == 1))
            ins.then_inc(sums_done, 1)

        def rest(h, s):
            for t in range(N_TILES):
                if t < N_TILES - 1:
                    pe.wait_ge(score_copied, h * N_TILES + t + START)
                else:
                    wait_apart(pe, score_copied, h * N_TILES + t + START, key_copied, PH)
                for j in range(2):
                    ins = nc.tensor.matmul(scores[0:width(t), t % 3, j * P:(j + 1) * P], q_t[:, s, j, t * P:t * P + width(t)],
                                           keys_t[:, bass.ds(h, 1), j, :].rearrange("p a n -> p (a n)"), start=True, stop=True)
                ins.then_inc(scored, 1)

        heads(pe, query, norm, rest)

    @block.vector
    def _(dve):
        order = Order(dve, own)
        link = order.link
        dve.wait_ge(keys_in, 48)
        for h in range(PH):
            dve.wait_ge(key_turned, h + 1)
            nc.vector.tensor_tensor(keys_t[:, h], turned[:], key_w[:].unsqueeze(2).broadcast_to([P, 2, P]), ALU.mult).then_inc(key_copied, 1)
        nc.vector.memset(mark[:], 0.0).then_inc(score_copied, 2)

        def query(h, i, s, j):
            if j == 0 and not (isinstance(h, int) and h < 2):
                dve.wait_ge(scored, h * N_TILES - N_TILES + START)
                dve.wait_ge(squared, h * 6 - 6 + START)
            for k, (t0, n) in enumerate(PIECES):
                dve.wait_ge(q_done, h * 6 + (3 * j + k + 1) + START)
                nc.vector.tensor_copy(q_t[:, s, j, t0:t0 + n], acc[:, k, 0:n]).then_inc(q_copied, 1)

        def norm(h, s):
            if not (isinstance(h, int) and h == 0):
                dve.wait_ge(score_copied, h * N_TILES + 2 + START)
            dve.wait_ge(roots_done, h + 1 + START)
            link(nc.vector.reciprocal(stat[:, 1, 0:N_TILES - 1], stat[:, 0, 0:N_TILES - 1]))
            nc.vector.reciprocal(stat[0:S_TOK, 1, N_TILES - 1:], stat[0:S_TOK, 0, N_TILES - 1:]).then_inc(rstd_done, 1)

        def rest(h, s):
            dve.wait_ge(rstd_done, h + 1 + START)
            for t in range(N_TILES):
                n_cols = width(t)
                dve.wait_ge(scored, h * N_TILES + (t + 1) + START)
                if not (isinstance(h, int) and h == 0):
                    dve.wait_ge(stored[t], h * 16 + START)
                nc.vector.tensor_scalar(stage[0:n_cols, t, :], scores[0:n_cols, t % 3, 0:QD], stat[0:n_cols, 1, t:t + 1], None,
                                        ALU.mult).then_inc(score_copied, 1)
            order.restart()

        heads(dve, query, norm, rest)

    @block.scalar
    def _(act):
        def query(h, i, s, j):
            if j == 0 and not (isinstance(h, int) and h < 2):
                act.wait_ge(sums_done, h - 1 + START)
            for k, (t0, n) in enumerate(PIECES):
                act.wait_ge(q_copied, h * 6 + (3 * j + k + 1))
                nc.scalar.activation(square[:, s, j, t0:t0 + n], q_t[:, s, j, t0:t0 + n], ACT.Square).then_inc(squared, 1)

        def norm(h, s):
            act.wait_ge(sums_done, h + 1 + START)
            if not (isinstance(h, int) and h == 0):
                act.wait_ge(rstd_done, h + START)
            nc.scalar.activation(stat[:, 0, 0:N_TILES - 1], sums[:, 0:N_TILES - 1], ACT.Sqrt, bias=const["eps"][:], scale=1.0 / QD)
            nc.scalar.activation(stat[0:S_TOK, 0, N_TILES - 1:], sums[0:S_TOK, N_TILES - 1:], ACT.Sqrt, bias=const["eps"][0:S_TOK, :],
                                 scale=1.0 / QD).then_inc(roots_done, 1)

        def rest(h, s):
            for t in range(N_TILES):
                act.wait_ge(score_copied, h * N_TILES + (t + 3) + START)
                n_cols = width(t)
                at = h * P + t * (PH * P) if t < N_TILES - 1 else h * S_TOK + t * (PH * P)
                act.dma_start(dram["scores"][bass.ds(at, n_cols), :], stage[0:n_cols, t, :]).then_inc(stored[t], 16)

        heads(act, query, norm, rest)
        for k in range(N_TILES):
            act.wait_ge(stored[k], 16 * PH + START)


def sample_constants():
    rows = np.arange(P) % S_TOK
    b, t = rows // DEC_T, rows % DEC_T
    nb, nt = np.arange(S_TOK) // DEC_T, np.arange(S_TOK) % DEC_T
    mask = np.zeros((P, len(GROUPS), P + S_TOK), np.float32)
    mask[:, 0, :P] = np.where(np.arange(P)[None] >= t[:, None], 0.0, MASKED)
    same = nb[None] == b[:, None]
    mask[:, 0, P:] = np.where(same & (nt[None] <= t[:, None]), 0.0, MASKED)
    mask[:, 1:, P:] = np.where(same & (nt[None] == t[:, None]), 0.0, MASKED)[:, None]
    return {"mask_sample": mask.reshape(P, -1)}


def peer_phase(nc, ctx, sem, const, x, dram, out_prompt, out_sample):
    sb = lambda name, shape, dt=F32: ctx.enter_context(nc.sbuf_tensor(name, shape, dt))
    psum = lambda name, shape: ctx.enter_context(nc.psum_tensor(name, shape, F32))
    FOLD = P // S_TOK
    S_FIRST = (N_TILES - 1) * PH
    N_STEPS = S_FIRST + PH // FOLD
    AHEAD = 2

    score_pair = sb("score_pair", [P, 2, N_KEYS])
    score_rest = sb("score_rest", [P, 2, N_KEYS])
    best_val = sb("best_val", [P, 2, TOPK])
    best_idx = sb("best_idx", [P, 2, TOPK], U32)
    best_idx_f = sb("best_idx_f", [P, 2, TOPK])
    cand = sb("cand", [P, TOPK, TOPK])
    cand_rest = sb("cand_rest", [P, TOPK, TOPK])
    top_val = sb("top_val", [P, TOPK])
    sel = sb("sel", [P, TOPK], U32)
    sel_halves = sb("sel_halves", [P, 2, TOPK], U32)
    sel_halves_f = sb("sel_halves_f", [P, 2, TOPK])
    onehot = sb("onehot", [P, 2, TOPK, TOPK])
    picked = sb("picked", [P, 2, TOPK])
    top_all = sb("top_all", [P, N_STEPS * TOPK])
    less_max = sb("less_max", [P, N_STEPS])
    exp_all = sb("exp_all", [P, N_STEPS * TOPK])
    den_all = sb("den_all", [P, N_STEPS])
    idx_all = sb("idx_all", [P, N_STEPS * TOPK], U32)
    weight_all = sb("weight_all", [P, N_STEPS * TOPK])
    idx_u_now = sb("idx_u_now", [P, TOPK], U32)
    idx_v_now = sb("idx_v_now", [P, TOPK], U32)
    act_now = sb("act_now", [P, TOPK])
    gelu_now = sb("gelu_now", [P, TOPK])
    den_now = sb("den_now", [P, 2])
    n2_rows = sb("n2_rows", [P, D])
    x1_rows = sb("x1_rows", [P, D])
    moe_sum = sb("moe_sum", [P, D])
    gate2_p = sb("gate2_p", [P, D])
    gate2_s = sb("gate2_s", [P, D])
    u_ring = sb("u_ring", [P, RING, D])
    v_ring = sb("v_ring", [P, RING, D])
    diag = sb("diag", [P, RING, P])
    fold = sb("fold", [P, S_TOK])
    acc = psum("peer_acc", [P, 2, 512])

    iota16, ident, zeros, consts_ready = const["iota16"], const["ident"], const["zeros"], const["ready"]
    scores_loaded = sem("scores_loaded")
    scores_read = sem("scores_read")
    picks_ready = sem("picks_ready")
    tops_ready = sem("tops_ready")
    exps_ready = sem("exps_ready")
    u_landed = [sem(f"u_landed{s}") for s in range(RING)]
    v_landed = [sem(f"v_landed{s}") for s in range(RING)]
    u_free = sem("u_free")
    v_free = sem("v_free")
    gelu_ready = sem("gelu_ready")
    weights_ready = sem("weights_ready")
    diag_ready = sem("diag_ready")
    sum_ready = sem("sum_ready")
    sum_copied = sem("sum_copied")
    n2_loaded = sem("n2_loaded")
    x1_loaded = sem("x1_loaded")
    gates_loaded = sem("gates_loaded")
    fold_ready = sem("fold_ready")
    y_ready = sem("y_ready")
    y_stored = sem("y_stored")
    dve_own = sem("peer_dve_own")
    pool_own = sem("peer_pool_own")
    act_own = sem("peer_act_own")

    of = lambda g: bass.ds(g * TOPK, TOPK)
    one = lambda g: bass.ds(g, 1)

    block = ctx.enter_context(nc.Block())

    @block.sync
    def _(sp):
        def load_scores(g):
            sp.dma_start(score_pair[:].rearrange("p a b -> p (a b)"),
                         dram["scores"][bass.ds(g * P, P), :]).then_inc(scores_loaded, 16)

        def load_scores_of(steps):
            with sp.Fori(steps[0], steps[1]) as g:
                sp.wait_ge(scores_read, g + AHEAD)
                load_scores(g + AHEAD)

        def load_n2(t, w):
            sp.dma_start(n2_rows[0:w, :], dram["n2"][bass.ds(t * P, w), :]).then_inc(n2_loaded, 16)

        def load_x1(t, w):
            sp.dma_start(x1_rows[0:w, :], dram["x1"][bass.ds(t * P, w), :]).then_inc(x1_loaded, 16)

        def turn_x1(t, w):
            sp.wait_ge(y_ready, t)
            sp.dma_start(out_prompt[bass.ds((t - 1) * P, P), :], x1_rows[:]).then_inc(y_stored, 16)
            sp.wait_ge(y_stored, 16 * t)
            load_x1(t, w)

        load_scores(0)
        sp.wait_ge(scores_read, 1)
        load_scores(1)
        load_n2(0, P)
        load_x1(0, P)
        sp.dma_start(gate2_p[:], dram["mod"][0:1, 5 * D:6 * D].broadcast_to([P, D])).then_inc(gates_loaded, 16)
        for b in range(DEC_B):
            sp.dma_start(gate2_s[b * DEC_T:(b + 1) * DEC_T, :],
                         dram["mod"][b + 1:b + 2, 5 * D:6 * D].broadcast_to([DEC_T, D])).then_inc(gates_loaded, 16)

        load_scores_of((0, PH))
        sp.wait_ge(u_free, RING + PH * TOPK)
        load_n2(1, P)
        with sp.Fori(1, N_TILES - 2) as t:
            load_scores_of((t * PH, t * PH + PH))
            sp.wait_ge(u_free, (t + 1) * (PH * TOPK) + RING)
            load_n2(t + 1, P)
            turn_x1(t, P)
        load_scores_of((S_FIRST - PH, S_FIRST))
        sp.wait_ge(u_free, S_FIRST * TOPK + RING)
        for k in range(FOLD):
            sp.dma_start(n2_rows[k * S_TOK:(k + 1) * S_TOK, :], dram["n2"][SEQ:TOK, :]).then_inc(n2_loaded, 16)
        turn_x1(N_TILES - 2, P)
        turn_x1(N_TILES - 1, S_TOK)
        sp.wait_ge(y_ready, N_TILES)
        sp.dma_start(out_sample, x1_rows[0:S_TOK, :]).then_inc(y_stored, 16)
        sp.wait_ge(y_stored, 16 * N_TILES)

    @block.gpsimd
    def _(pool):
        def gathers(u, v):
            for k in range(TOPK):
                if k % RING == 0:
                    half = slice(k, k + RING)
                    if u is not None:
                        pool.wait_ge(picks_ready, u + 1)
                        nc.gpsimd.tensor_copy(idx_u_now[:, half], idx_all[:, bass.ds(u * TOPK + k, RING)]).then_inc(pool_own, 1)
                    if v is not None:
                        nc.gpsimd.tensor_copy(idx_v_now[:, half], idx_all[:, bass.ds(v * TOPK + k, RING)]).then_inc(pool_own, 1)
                    pool.wait_ge(pool_own, (u is not None) + (v is not None))
                    pool.sem_clear(pool_own)
                if u is not None:
                    wait_apart(pool, u_free, u * TOPK + (k + 1), consts_ready, 3)
                    nc.gpsimd.indirect_dma_start(
                        u_ring[:, k % RING, :], None, x["peer_u"][0],
                        bass.IndirectOffsetOnAxis(ap=idx_u_now[:, k:k + 1], axis=0)).then_inc(u_landed[k % RING], 16)
                if v is not None:
                    wait_apart(pool, v_free, v * TOPK + (k + 1), consts_ready, 3)
                    nc.gpsimd.indirect_dma_start(
                        v_ring[:, k % RING, :], None, x["peer_v"][0],
                        bass.IndirectOffsetOnAxis(ap=idx_v_now[:, k:k + 1], axis=0)).then_inc(v_landed[k % RING], 16)

        gathers(0, None)
        with pool.Fori(1, N_STEPS) as g:
            gathers(g, g - 1)
        gathers(None, N_STEPS - 1)

    @block.vector
    def _(dve):
        own = [0]

        def link(ins):
            own[0] += 1
            ins.then_inc(dve_own, 1)
            dve.wait_ge(dve_own, own[0])

        def relink():
            dve.sem_clear(dve_own)
            own[0] = 0

        nc.vector.memset(act_now[:], 0.0).then_inc(u_free, RING)
        dve.wait_ge(consts_ready, 3)
        link(nc.vector.tensor_copy(fold[:], ident[:, 0:S_TOK]))
        for k in range(1, FOLD):
            ins = nc.vector.tensor_tensor(fold[:], fold[:], ident[:, k * S_TOK:(k + 1) * S_TOK], ALU.add)
            if k < FOLD - 1:
                link(ins)
        ins.then_inc(fold_ready, 1)

        def pick_experts(g):
            wait_apart(dve, scores_loaded, g * 16 + 16, consts_ready, 3)
            for j in range(2):
                link(nc.vector.max(best_val[:, j, 0:8], score_pair[:, j, :]))
                nc.vector.max_index(best_idx[:, j, 0:8], best_val[:, j, 0:8], score_pair[:, j, :])
                link(nc.vector.match_replace(score_rest[:, j, :], best_val[:, j, 0:8], score_pair[:, j, :], LOWEST))
                link(nc.vector.max(best_val[:, j, 8:16], score_rest[:, j, :]))
                link(nc.vector.max_index(best_idx[:, j, 8:16], best_val[:, j, 8:16], score_rest[:, j, :]))
            nc.vector.tensor_copy(best_idx_f[:], best_idx[:]).then_inc(scores_read, 1)
            link(nc.vector.tensor_tensor(
                cand[:], best_val[:, 0, :].unsqueeze(2).broadcast_to([P, TOPK, TOPK]),
                best_val[:, 1, :].unsqueeze(1).broadcast_to([P, TOPK, TOPK]), ALU.add))
            flat = cand[:].rearrange("p a b -> p (a b)")
            flat_rest = cand_rest[:].rearrange("p a b -> p (a b)")
            link(nc.vector.max(top_val[:, 0:8], flat))
            nc.vector.max_index(sel[:, 0:8], top_val[:, 0:8], flat)
            link(nc.vector.match_replace(flat_rest, top_val[:, 0:8], flat, LOWEST))
            link(nc.vector.max(top_val[:, 8:16], flat_rest))
            link(nc.vector.max_index(sel[:, 8:16], top_val[:, 8:16], flat_rest))
            nc.vector.tensor_copy(top_all[:, of(g)], top_val[:, :])
            nc.vector.tensor_scalar(less_max[:, one(g)], top_val[:, 0:1], -1.0, None, ALU.mult).then_inc(tops_ready, 1)
            nc.vector.tensor_scalar(sel_halves[:, 0, :], sel[:, :], 4, None, ALU.logical_shift_right)
            link(nc.vector.tensor_scalar(sel_halves[:, 1, :], sel[:, :], 15, None, ALU.bitwise_and))
            link(nc.vector.tensor_copy(sel_halves_f[:], sel_halves[:]))
            for j in range(2):
                link(nc.vector.tensor_tensor(
                    onehot[:, j], sel_halves_f[:, j].unsqueeze(2).broadcast_to([P, TOPK, TOPK]),
                    iota16[:].unsqueeze(1).broadcast_to([P, TOPK, TOPK]), ALU.is_equal))
            for j in range(2):
                link(nc.vector.tensor_tensor(
                    onehot[:, j], onehot[:, j],
                    best_idx_f[:, j].unsqueeze(1).broadcast_to([P, TOPK, TOPK]), ALU.mult))
            link(nc.vector.tensor_reduce(picked[:], onehot[:], AX_X, ALU.add))
            nc.vector.scalar_tensor_tensor(
                out=idx_all[:, of(g)], in0=picked[:, 0, :], scalar=float(N_KEYS),
                in1=picked[:, 1, :], op0=ALU.mult, op1=ALU.add).then_inc(picks_ready, 1)

        def dots(g):
            for k in range(TOPK):
                dve.wait_ge(u_landed[k % RING], g * (16 * TOPK // RING) + (k // RING + 1) * 16)
                nc.vector.scalar_tensor_tensor(
                    out=u_ring[:, k % RING, :], in0=u_ring[:, k % RING, :], scalar=1.0, in1=n2_rows[:, :],
                    op0=ALU.mult, op1=ALU.mult, accum_out=act_now[:, k:k + 1]).then_inc(u_free, 1)

        def weights(g):
            dve.wait_ge(exps_ready, g + 1)
            link(nc.vector.reciprocal(den_now[:, 0:1], den_all[:, one(g)]))
            dve.wait_ge(gelu_ready, g + 1)
            nc.vector.scalar_tensor_tensor(
                out=weight_all[:, of(g)], in0=gelu_now[:, :], scalar=den_now[:, 0:1], in1=exp_all[:, of(g)],
                op0=ALU.mult, op1=ALU.mult).then_inc(weights_ready, 1)
            dve.wait_ge(weights_ready, g + 1)

        def steps(first, end, pick):
            with dve.Fori(first, end) as g:
                dots(g)
                if pick:
                    pick_experts(g + AHEAD)
                weights(g)
                link(nc.vector.tensor_copy(den_now[:, 1:2], den_now[:, 0:1]))
                relink()

        def residual(t, w, gate):
            wait_apart(dve, x1_loaded, 16 * t + 16, consts_ready, 3)
            dve.wait_ge(sum_copied, t + 1)
            link(nc.vector.tensor_tensor(moe_sum[0:w, :], moe_sum[0:w, :], gate[0:w, :], ALU.mult))
            nc.vector.tensor_tensor(x1_rows[0:w, :], x1_rows[0:w, :], moe_sum[0:w, :], ALU.add).then_inc(y_ready, 1)
            relink()

        for g in range(AHEAD):
            pick_experts(g)
        relink()
        wait_apart(dve, gates_loaded, 16 * (1 + DEC_B), consts_ready, 3)
        dve.wait_ge(n2_loaded, 16)
        steps(0, PH, True)
        with dve.Fori(1, N_TILES - 1) as t:
            wait_apart(dve, n2_loaded, t * 16 + 16, consts_ready, 3)
            steps(t * PH, t * PH + PH, True)
            residual(t - 1, P, gate2_p)
        dve.wait_ge(n2_loaded, (N_TILES - 1 + FOLD) * 16)
        steps(S_FIRST, N_STEPS, False)
        residual(N_TILES - 2, P, gate2_p)
        residual(N_TILES - 1, S_TOK, gate2_s)

    @block.scalar
    def _(act):
        act.wait_ge(consts_ready, 3)

        def exps(g):
            act.wait_ge(tops_ready, g + 1)
            nc.scalar.activation(exp_all[:, of(g)], top_all[:, of(g)], ACT.Exp, bias=less_max[:, one(g)],
                                 accum_out=den_all[:, one(g)]).then_inc(exps_ready, 1)

        def steps(first, end, pattern, more):
            with act.Fori(first, end) as g:
                if more:
                    exps(g + 1)
                act.wait_ge(u_free, g * TOPK + (TOPK + RING))
                nc.scalar.activation(gelu_now[:], act_now[:], ACT.Gelu_apprx_tanh).then_inc(gelu_ready, 1)
                act.wait_ge(weights_ready, g + 1)
                for k in range(TOPK):
                    act.wait_ge(v_free, g * TOPK + (k + 1))
                    nc.scalar.activation(diag[:, k % RING, 0:pattern.shape[1]], pattern[:], ACT.Copy,
                                         scale=weight_all[:, bass.ds(g * TOPK + k, 1)]).then_inc(diag_ready, 1)

        def copy_sum(t, w):
            act.wait_ge(sum_ready, t + 1)
            if not (isinstance(t, int) and t == 0):
                act.wait_ge(y_ready, t)
            nc.scalar.activation(moe_sum[0:w, :], acc[0:w].rearrange("p a b -> p (a b)"), ACT.Copy).then_inc(sum_copied, 1)

        exps(0)
        steps(0, PH, ident, True)
        copy_sum(0, P)
        with act.Fori(1, N_TILES - 1) as t:
            steps(t * PH, t * PH + PH, ident, True)
            copy_sum(t, P)
        act.wait_ge(fold_ready, 1)
        steps(S_FIRST, N_STEPS - 1, fold, True)
        steps(N_STEPS - 1, N_STEPS, fold, False)
        copy_sum(N_TILES - 1, S_TOK)

    @block.tensor
    def _(pe):
        pe.wait_ge(consts_ready, 3)

        def tile(t, first, end, w):
            if isinstance(t, int) and t == 0:
                nc.tensor.matmul(acc[:, 0, :], zeros[:, 0:P], zeros[:, :], start=True, stop=False)
                nc.tensor.matmul(acc[:, 1, :], zeros[:, 0:P], zeros[:, :], start=True, stop=False).then_inc(v_free, RING)
            else:
                pe.wait_ge(sum_copied, t)
                for c in range(2):
                    nc.tensor.matmul(acc[:, c, :], zeros[:, 0:P], zeros[:, :], start=True, stop=False)
            with pe.Fori(first, end) as g:
                for k in range(TOPK):
                    pe.wait_ge(diag_ready, g * TOPK + (k + 1))
                    pe.wait_ge(v_landed[k % RING], g * (16 * TOPK // RING) + (k // RING + 1) * 16)
                    for c in range(2):
                        ins = nc.tensor.matmul(acc[0:w, c, :], diag[:, k % RING, 0:w], v_ring[:, k % RING, c * 512:(c + 1) * 512],
                                               start=False, stop=False)
                    ins.then_inc(v_free, 1)
            for c in range(2):
                ins = nc.tensor.matmul(acc[:, c, :], zeros[:, 0:P], zeros[:, :], start=False, stop=True)
            ins.then_inc(sum_ready, 1)

        tile(0, 0, PH, P)
        with pe.Fori(1, N_TILES - 1) as t:
            tile(t, t * PH, t * PH + PH, P)
        tile(N_TILES - 1, S_FIRST, N_STEPS, S_TOK)


def build(nc, x, consts, outs):
    y_p, y_s, kv1_p, kv2_p, kv3_p, state_p, kv1_s, kv2_s, kv3_s, state_s = outs
    scratch = lambda name, shape: nc.dram_tensor(name, shape, F32, kind="Internal").ap()
    dram = {
        "mod": scratch("mod", [1 + DEC_B, 6 * D]),
        "h_t": scratch("h_t", [T_GATE + 2 * D, TOK]),
        "h_r": scratch("h_r", [TOK, R_V + 3 * WIDTH]),
        "oa_t": scratch("oa_t", [WIDTH, TOK]),
        "ob_t": scratch("ob_t", [WIDTH, TOK]),
        "qk": scratch("qk_rows_dram", [TOK, 6 * WIDTH]),
        "att": scratch("att", [len(GROUPS), SEQ, HEADS * (DH + 2)]),
        "x1": scratch("x1", [TOK, D]),
        "n2": scratch("n2", [TOK, D]),
        "scores": scratch("scores", [TOK * PH, 2 * N_KEYS]),
    }
    x_s = x["x_sample"].rearrange("b t d -> (b t) d")
    x_rows = lambda n, w: x_s if w == S_TOK else x["x_prompt"][0][bass.ds(n * P, P), :]
    x1_rows = lambda n, w: dram["x1"][bass.ds(n * P, w), :]
    n2_rows = lambda n, w: dram["n2"][bass.ds(n * P, w), :]
    with ExitStack() as whole:
        held = []

        def sem(name, start=0):
            held.append(nc.alloc_semaphore(name=name))
            if start:
                nc.sync.sem_inc(held[-1], start)
            return held[-1]

        def phase(run, *args):
            with ExitStack() as ctx:
                run(nc, ctx, sem, const, *args)
            nc.clear_and_free_semaphores(held)
            nc.all_engine_barrier()
            held.clear()

        keep = lambda name, shape: whole.enter_context(nc.sbuf_tensor(name, shape, F32))
        const = {"ident": keep("ident", [P, P]), "zeros": keep("zeros", [P, BLOCK]), "ones": keep("ones", [P, P]),
                 "eps": keep("eps", [P, 1]), "iota16": keep("iota16", [P, TOPK]), "ready": nc.alloc_semaphore(name="consts_ready")}
        consts_phase(nc, sem, const)
        phase(mod_phase, x, dram)
        with nc.sbuf_tensor("n1_hi", [P, DC, TOK], F32R) as n1_hi, nc.sbuf_tensor("n1_lo", [P, DC, TOK], F32R) as n1_lo:
            phase(norm_phase, "_1", x_rows, x["norm1_w"], dram["mod"], 0, D, n1_hi, n1_lo, None)
            phase(project_phase, n1_hi, n1_lo, x, consts, dram, state_p, state_s)
        caches = [x["cache_kv_g1"][0], x["cache_kv_g2"][0], x["cache_kv_g3"][0]]
        with nc.sbuf_tensor("qk_t", [P, 6 * HEADS, TOK], F32) as qk_t, \
                nc.sbuf_tensor("scores_t", [P, len(GROUPS), HEADS, DEC_B, DEC_T], F32) as s_t:
            phase(rotate_phase, x, consts, dram, qk_t)
            phase(attention_phase, consts, dram, qk_t, caches, s_t, (kv1_p, kv2_p, kv3_p), (kv1_s, kv2_s, kv3_s))
            phase(merge_phase, caches, consts, dram, qk_t, s_t)
        phase(mix_phase, x, dram, x_rows)
        with nc.sbuf_tensor("n2_hi", [P, DC, TOK], F32R) as n2_hi, nc.sbuf_tensor("n2_lo", [P, DC, TOK], F32R) as n2_lo:
            phase(norm_phase, "_2", x1_rows, x["norm2_w"], dram["mod"], 3 * D, 4 * D, n2_hi, n2_lo, n2_rows)
            phase(query_phase, x, dram, n2_hi, n2_lo)
        phase(peer_phase, x, dram, y_p[0], y_s.rearrange("b t d -> (b t) d"))


INPUTS = ["x_prompt", "x_sample", "cache_kv_g1", "cache_kv_g2", "cache_kv_g3", "state_hgrn", "c_prompt", "c_sample",
          "w_ada", "b_ada", "norm1_w", "norm2_w", "w_in", "lb_logits", "hgrn_norm_w", "q_norm_w", "k_norm_w",
          "w_branch_a", "w_branch_b", "w_out", "peer_wq", "peer_qn_w", "peer_k1", "peer_k2", "peer_u", "peer_v"]
OUTPUTS = [(1, SEQ, D), (DEC_B, DEC_T, D)] + [(1, 1, 2, HEADS, min(w, SEQ), DH) for w, _ in GROUPS] + \
    [(1, 1, HEADS, DH, DH)] + [(1, DEC_B, 2, HEADS, DEC_T, DH)] * 3 + [(1, DEC_B, HEADS, DH, DH)]


def kernel(**inputs):
    import concourse.bacc as bacc
    from concourse.bass_utils import run_bass_kernel_spmd

    nc = bacc.Bacc("TRN2", target_bir_lowering=False, num_devices=1)
    arrays, x, consts = {}, {}, {}
    for name in INPUTS:
        a = np.ascontiguousarray(inputs[name])
        arrays["in_" + name] = a
        x[name] = nc.dram_tensor("in_" + name, a.shape, mybir.dt.from_np(a.dtype), kind="ExternalInput").ap()
    for name, a in {**shape_constants(), **attention_constants(), **sample_constants()}.items():
        arrays["c_" + name] = a
        consts[name] = nc.dram_tensor("c_" + name, a.shape, mybir.dt.from_np(a.dtype), kind="ExternalInput").ap()
    outs = [nc.dram_tensor(f"out_{i}", shape, F32, kind="ExternalOutput").ap() for i, shape in enumerate(OUTPUTS)]
    build(nc, x, consts, outs)
    r = run_bass_kernel_spmd(nc, [arrays], core_ids=[0])
    return tuple(r.results[0][f"out_{i}"] for i in range(len(OUTPUTS)))
```
